# Optimizing a Trainium2 kernel written in Bass

```python
import jax, jax.numpy as jnp
from jax import lax
import numpy as np

D_MODEL = 2048
BATCH = 1
SEQ = 256
DEPTH = 1
DEC_BATCH = 8
DEC_SEQ = 8
PAST_LEN = 256
PAGE_SIZE = 128

NSA_HEADS = 8
NSA_GROUPS = 2
NSA_HPG = NSA_HEADS // NSA_GROUPS
NSA_HD = 128
NSA_BLOCK = 64
NSA_TOPN = 8
NSA_WINDOW = 512
Q_BLOCK = 128
NSA_SCALE = NSA_HD ** -0.5
FORCED_SCORE = NSA_HPG + 1.0
HG_HEADS = 8
HG_DK = 128
HG_DV = 128
HG_CHUNK = 16
D_FF = 5632
CONV_W = 3
EPS = 1e-6
IN_SIZES = (NSA_HEADS * NSA_HD, 2 * NSA_GROUPS * NSA_HD, 2 * NSA_GROUPS * NSA_HD, 2 * NSA_GROUPS * NSA_HD, 3 * NSA_HEADS, HG_HEADS * HG_DK, HG_HEADS * HG_DK, HG_HEADS * HG_DV, HG_HEADS * HG_DV, 2 * D_MODEL)
IN_COLS = sum(IN_SIZES)

kernel_name = 'nsa_hgrn2_gated_hybrid_decode_step'

def rmsnorm(x, w):
    xf = x.astype(jnp.float32)
    y = xf * lax.rsqrt(jnp.mean(xf * xf, axis=-1, keepdims=True) + EPS)
    return (y * w.astype(jnp.float32)).astype(x.dtype)

def masked_softmax(s, mask):
    s = jnp.where(mask, s.astype(jnp.float32), -jnp.inf)
    m = jnp.max(s, axis=-1, keepdims=True)
    m = jnp.where(jnp.isfinite(m), m, 0.0)
    e = jnp.where(mask, jnp.exp(s - m), 0.0)
    d = jnp.sum(e, axis=-1, keepdims=True)
    return e / jnp.where(d > 0, d, 1.0)

def alibi_slopes():
    h = jnp.arange(NSA_HEADS, dtype=jnp.float32)
    return jnp.exp2(-8.0 * (h + 1.0) / NSA_HEADS).reshape(NSA_GROUPS, NSA_HPG)

def compress_blocks(kv, pe, w1, w2):
    b, length = kv.shape[:2]
    n_cmp = length // NSA_BLOCK
    kc = kv[:, :n_cmp * NSA_BLOCK].reshape(b, n_cmp, NSA_BLOCK, 2, NSA_GROUPS, NSA_HD)
    hid = jax.nn.silu(jnp.einsum('bnlcgd,lcde->bncge', kc + pe[:, :, None, :], w1))
    out = jnp.einsum('bncge,cef->bncgf', hid, w2)
    return out[:, :, 0], out[:, :, 1]

def nsa_local(qg, q_pos, idx, kb, kv_win, k_pos_win, slopes):
    b, t = qg.shape[:2]
    n_sel = idx.shape[-1]
    idx_t = idx.transpose(0, 2, 1, 3)
    gath = jax.vmap(jax.vmap(lambda kbg, ig: kbg[ig]))(kb, idx_t)
    kpos = idx_t[..., None] * NSA_BLOCK + jnp.arange(NSA_BLOCK)
    dist = (q_pos[None, None, :, None, None] - kpos).astype(jnp.float32)
    s = jnp.einsum('btghd,bgtnsd->bgthns', qg, gath[..., 0, :]).astype(jnp.float32) * NSA_SCALE
    s = s - slopes[None, :, None, :, None, None] * dist[:, :, :, None]
    n_keys = n_sel * NSA_BLOCK
    p = masked_softmax(s.reshape(b, NSA_GROUPS, t, NSA_HPG, n_keys), (dist >= 0).reshape(b, NSA_GROUPS, t, 1, n_keys))
    o_sel = jnp.einsum('bgthk,bgtkd->btghd', p.astype(qg.dtype), gath[..., 1, :].reshape(b, NSA_GROUPS, t, n_keys, NSA_HD))
    dist_w = q_pos[:, None] - k_pos_win[None, :]
    mask_w = (k_pos_win[None, :] >= 0) & (dist_w >= 0) & (dist_w < NSA_WINDOW)
    s_w = jnp.einsum('btghd,bsgd->btghs', qg, kv_win[:, :, 0]).astype(jnp.float32) * NSA_SCALE
    s_w = s_w - slopes[None, None, :, :, None] * dist_w.astype(jnp.float32)[:, None, None, :]
    p_w = masked_softmax(s_w, mask_w[:, None, None, :])
    o_win = jnp.einsum('btghs,bsgd->btghd', p_w.astype(qg.dtype), kv_win[:, :, 1])
    return o_sel, o_win

def nsa_mixer(qg, kvc_full, kvs_full, win_src, win_pos, q_pos, gate_logits, pe, w1, w2, blocked):
    b, t = qg.shape[:2]
    length = kvc_full.shape[1]
    slopes = alibi_slopes()
    ck, cv = compress_blocks(kvc_full, pe, w1, w2)
    n_cmp = ck.shape[1]
    ends = (jnp.arange(n_cmp) + 1) * NSA_BLOCK - 1
    dist_c = q_pos[:, None] - ends[None, :]
    s_c = jnp.einsum('btghd,bngd->btghn', qg, ck).astype(jnp.float32) * NSA_SCALE
    s_c = s_c - slopes[None, None, :, :, None] * dist_c.astype(jnp.float32)[:, None, None, :]
    p_c = masked_softmax(s_c, (dist_c >= 0)[:, None, None, :])
    o_cmp = jnp.einsum('btghn,bngd->btghd', p_c.astype(cv.dtype), cv)
    n_blk = -(-length // NSA_BLOCK)
    imp = jnp.pad(p_c.sum(axis=3), ((0, 0), (0, 0), (0, 0), (0, n_blk - n_cmp)))
    cur = q_pos // NSA_BLOCK
    blk = jnp.arange(n_blk)
    forced = (blk[None, :] == 0) | (blk[None, :] == cur[:, None]) | (blk[None, :] == cur[:, None] - 1)
    valid = blk[None, :] <= cur[:, None]
    score = jnp.where(valid[None, :, None, :], jnp.where(forced[None, :, None, :], FORCED_SCORE, imp), -1.0)
    n_sel = min(NSA_TOPN, n_blk)
    _, idx = lax.top_k(score, n_sel)
    kvs_pad = jnp.pad(kvs_full, ((0, 0), (0, n_blk * NSA_BLOCK - length), (0, 0), (0, 0), (0, 0)))
    kb = kvs_pad.reshape(b, n_blk, NSA_BLOCK, 2, NSA_GROUPS, NSA_HD).transpose(0, 4, 1, 2, 3, 5)
    if blocked:
        nq = t // Q_BLOCK
        n_span = NSA_WINDOW // Q_BLOCK + 1
        padded = jnp.pad(win_src, ((0, 0), (NSA_WINDOW, 0), (0, 0), (0, 0), (0, 0)))
        pb = padded.reshape(b, nq + n_span - 1, Q_BLOCK, 2, NSA_GROUPS, NSA_HD)
        spans = jnp.stack([pb[:, i:i + nq] for i in range(n_span)], axis=2).reshape(b, nq, n_span * Q_BLOCK, 2, NSA_GROUPS, NSA_HD)
        span_pos = jnp.arange(nq)[:, None] * Q_BLOCK - NSA_WINDOW + jnp.arange(n_span * Q_BLOCK)[None, :]
        xs = (qg.reshape(b, nq, Q_BLOCK, NSA_GROUPS, NSA_HPG, NSA_HD).transpose(1, 0, 2, 3, 4, 5),
              q_pos.reshape(nq, Q_BLOCK),
              idx.reshape(b, nq, Q_BLOCK, NSA_GROUPS, n_sel).transpose(1, 0, 2, 3, 4),
              spans.transpose(1, 0, 2, 3, 4, 5),
              span_pos)
        o_sel, o_win = lax.map(lambda a: nsa_local(a[0], a[1], a[2], kb, a[3], a[4], slopes), xs)
        o_sel = o_sel.transpose(1, 0, 2, 3, 4, 5).reshape(b, t, NSA_GROUPS, NSA_HPG, NSA_HD)
        o_win = o_win.transpose(1, 0, 2, 3, 4, 5).reshape(b, t, NSA_GROUPS, NSA_HPG, NSA_HD)
    else:
        o_sel, o_win = nsa_local(qg, q_pos, idx, kb, win_src, win_pos, slopes)
    g = jax.nn.sigmoid(gate_logits.astype(jnp.float32)).reshape(b, t, NSA_GROUPS, NSA_HPG, 3).astype(qg.dtype)
    o = g[..., 0:1] * o_cmp + g[..., 1:2] * o_sel + g[..., 2:3] * o_win
    return o.reshape(b, t, NSA_HEADS * NSA_HD)

def hgrn2_chunked(q, k, v, g, s0):
    b, t, h, dk = q.shape
    dv = v.shape[-1]
    pad = (-t) % HG_CHUNK
    n = (t + pad) // HG_CHUNK

    def blocks(a):
        a = jnp.pad(a.astype(jnp.float32), ((0, 0), (0, pad), (0, 0), (0, 0)))
        return a.reshape(b, n, HG_CHUNK, h, a.shape[-1]).transpose(1, 0, 2, 3, 4)

    qc, kc, vc, gc = blocks(q), blocks(k), blocks(v), blocks(g)
    cum = jnp.cumsum(gc, axis=2)
    last = cum[:, :, -1]
    q_dec = qc * jnp.exp(cum)
    k_inv = kc * jnp.exp(-cum)
    k_end = kc * jnp.exp(last[:, :, None] - cum)
    causal = jnp.tril(jnp.ones((HG_CHUNK, HG_CHUNK), dtype=bool))
    att = jnp.where(causal, jnp.einsum('nbthk,nbshk->nbhts', q_dec, k_inv), 0.0)
    o_intra = jnp.einsum('nbhts,nbshv->nbthv', att, vc)

    def step(s, xs):
        qd, ke, vv, la = xs
        o = jnp.einsum('bthk,bhkv->bthv', qd, s)
        s = jnp.exp(la)[..., None] * s + jnp.einsum('bshk,bshv->bhkv', ke, vv)
        return s, o

    s_fin, o_inter = lax.scan(step, s0.astype(jnp.float32), (q_dec, k_end, vc, last))
    o = (o_intra + o_inter).transpose(1, 0, 2, 3, 4).reshape(b, n * HG_CHUNK, h, dv)[:, :t]
    return o, s_fin

def conv_ffn(h, buf, w_up, cw, cb, w_dn):
    t = h.shape[1]
    u = h @ w_up
    full = jnp.concatenate([buf.astype(u.dtype), u], axis=1)
    c = cb
    for j in range(CONV_W):
        c = c + full[:, j:j + t] * cw[j]
    a, gt = jnp.split(c, 2, axis=-1)
    out = (jax.nn.gelu(gt, approximate=True) * a) @ w_dn
    return out, full[:, t:]

def decoder_layer(x, past, q_pos0, lb, params):
    (w_in, w_a, w_b, w_o, pe, w1, w2, hg_norm, ln1, ln2, ln3, ln4, w_up, cw, cb, w_dn) = params
    b, t, _ = x.shape
    h = rmsnorm(x, ln1)
    splits = [int(v) for v in np.cumsum(IN_SIZES)[:-1]]
    (q_a, kvc, kvs, kvw, g_nsa, q_b, f_b, i_b, og_b, g_mrg) = jnp.split(h @ w_in, splits, axis=-1)
    kv_shape = (b, t, 2, NSA_GROUPS, NSA_HD)
    kvc, kvs, kvw = kvc.reshape(kv_shape), kvs.reshape(kv_shape), kvw.reshape(kv_shape)
    qg = q_a.reshape(b, t, NSA_GROUPS, NSA_HPG, NSA_HD)
    q_pos = q_pos0 + jnp.arange(t)
    if past is None:
        kvc_full, kvs_full, win_src, win_pos = kvc, kvs, kvw, None
        new_win = kvw[:, t - min(NSA_WINDOW, t):]
        s0 = jnp.zeros((b, HG_HEADS, HG_DK, HG_DV), jnp.float32)
        conv_buf = jnp.zeros((b, CONV_W - 1, 2 * D_FF), x.dtype)
    else:
        past_c, past_s, win_buf, s0, conv_buf = past
        kvc_full = jnp.concatenate([past_c.astype(kvc.dtype), kvc], axis=1)
        kvs_full = jnp.concatenate([past_s.astype(kvs.dtype), kvs], axis=1)
        n_buf = win_buf.shape[1]
        win_src = jnp.concatenate([win_buf.astype(kvw.dtype), kvw], axis=1)
        win_pos = q_pos0 - n_buf + jnp.arange(n_buf + t)
        new_win = win_src[:, t:]
    o_a = nsa_mixer(qg, kvc_full, kvs_full, win_src, win_pos, q_pos, g_nsa, pe, w1, w2, past is None)
    f_raw = f_b.reshape(b, t, HG_HEADS, HG_DK).astype(jnp.float32)
    lbh = lb.reshape(HG_HEADS, HG_DK)
    forget = lbh + (1.0 - lbh) * jax.nn.sigmoid(f_raw)
    in_gate = (1.0 - lbh) * jax.nn.sigmoid(-f_raw)
    o_hg, s_fin = hgrn2_chunked(q_b.reshape(b, t, HG_HEADS, HG_DK), in_gate, i_b.reshape(b, t, HG_HEADS, HG_DV), jnp.log(forget), s0)
    o_hg = rmsnorm(o_hg, hg_norm).reshape(b, t, HG_HEADS * HG_DV).astype(x.dtype) * jax.nn.silu(og_b)
    ga, gb = jnp.split(g_mrg, 2, axis=-1)
    mixed = (jax.nn.sigmoid(ga) * (o_a @ w_a) + jax.nn.sigmoid(gb) * (o_hg @ w_b)) @ w_o
    x1 = x + rmsnorm(mixed, ln2)
    ffn, new_conv = conv_ffn(rmsnorm(x1, ln3), conv_buf, w_up, cw, cb, w_dn)
    y = x1 + rmsnorm(ffn, ln4)
    return y, (kvc, kvs, new_win, s_fin.astype(x.dtype), new_conv)

def setup_inputs(seed: int = 0) -> dict:
    key = jax.random.key(seed)
    ks = jax.random.split(key, 32)
    n_pages = PAST_LEN // PAGE_SIZE
    n_used = DEC_BATCH * n_pages
    n_phys = n_used + n_used // 4
    n_buf = min(NSA_WINDOW, PAST_LEN)

    def nrm(k, shape, scale):
        return jax.random.normal(k, shape, jnp.float32) * scale

    page_table = jax.random.permutation(ks[7], n_phys)[:n_used].reshape(DEC_BATCH, n_pages).astype(jnp.int32)
    kv_tail = (2, NSA_GROUPS, NSA_HD)
    return {
        'x_prompt': nrm(ks[0], (BATCH, SEQ, D_MODEL), 1.0),
        'x_sample': nrm(ks[1], (DEC_BATCH, DEC_SEQ, D_MODEL), 1.0),
        'cache_cmp_kv': nrm(ks[2], (DEPTH, n_phys, PAGE_SIZE) + kv_tail, 1.0),
        'cache_sel_kv': nrm(ks[3], (DEPTH, n_phys, PAGE_SIZE) + kv_tail, 1.0),
        'state_win_kv': nrm(ks[4], (DEPTH, DEC_BATCH, n_buf) + kv_tail, 1.0),
        'state_hgrn': nrm(ks[5], (DEPTH, DEC_BATCH, HG_HEADS, HG_DK, HG_DV), 0.5),
        'state_conv': nrm(ks[6], (DEPTH, DEC_BATCH, CONV_W - 1, 2 * D_FF), 1.0),
        'page_table': page_table,
        'w_in': nrm(ks[8], (DEPTH, D_MODEL, IN_COLS), D_MODEL ** -0.5),
        'w_branch_a': nrm(ks[9], (DEPTH, NSA_HEADS * NSA_HD, D_MODEL), (NSA_HEADS * NSA_HD) ** -0.5),
        'w_branch_b': nrm(ks[10], (DEPTH, HG_HEADS * HG_DV, D_MODEL), (HG_HEADS * HG_DV) ** -0.5),
        'w_out': nrm(ks[11], (DEPTH, D_MODEL, D_MODEL), D_MODEL ** -0.5),
        'cmp_pe': nrm(ks[12], (DEPTH, NSA_BLOCK, 2, NSA_HD), 0.1),
        'cmp_w1': nrm(ks[13], (DEPTH, NSA_BLOCK, 2, NSA_HD, NSA_HD), (NSA_BLOCK * NSA_HD) ** -0.5),
        'cmp_w2': nrm(ks[14], (DEPTH, 2, NSA_HD, NSA_HD), NSA_HD ** -0.5),
        'hg_lb_raw': nrm(ks[15], (DEPTH + 1, HG_HEADS * HG_DK), 0.5),
        'hg_norm_w': 1.0 + nrm(ks[16], (DEPTH, HG_DV), 0.02),
        'ln_mix_pre': 1.0 + nrm(ks[17], (DEPTH, D_MODEL), 0.02),
        'ln_mix_post': 1.0 + nrm(ks[18], (DEPTH, D_MODEL), 0.02),
        'ln_ffn_pre': 1.0 + nrm(ks[19], (DEPTH, D_MODEL), 0.02),
        'ln_ffn_post': 1.0 + nrm(ks[20], (DEPTH, D_MODEL), 0.02),
        'w_up': nrm(ks[21], (DEPTH, D_MODEL, 2 * D_FF), D_MODEL ** -0.5),
        'conv_w': nrm(ks[22], (DEPTH, CONV_W, 2 * D_FF), CONV_W ** -0.5),
        'conv_b': nrm(ks[23], (DEPTH, 2 * D_FF), 0.01),
        'w_down': nrm(ks[24], (DEPTH, D_FF, D_MODEL), D_FF ** -0.5),
    }

def reference(x_prompt, x_sample, cache_cmp_kv, cache_sel_kv, state_win_kv, state_hgrn, state_conv, page_table, w_in, w_branch_a, w_branch_b, w_out, cmp_pe, cmp_w1, cmp_w2, hg_lb_raw, hg_norm_w, ln_mix_pre, ln_mix_post, ln_ffn_pre, ln_ffn_post, w_up, conv_w, conv_b, w_down):
    dec_b, n_pages = page_table.shape
    past_len = n_pages * cache_cmp_kv.shape[2]
    lb_all = jnp.cumsum(jax.nn.softmax(hg_lb_raw.astype(jnp.float32), axis=0), axis=0)
    y_p, y_s = x_prompt, x_sample
    new_p, new_s = [], []
    for l in range(DEPTH):
        params = (w_in[l], w_branch_a[l], w_branch_b[l], w_out[l], cmp_pe[l], cmp_w1[l], cmp_w2[l], hg_norm_w[l],
                  ln_mix_pre[l], ln_mix_post[l], ln_ffn_pre[l], ln_ffn_post[l], w_up[l], conv_w[l], conv_b[l], w_down[l])
        y_p, st_p = decoder_layer(y_p, None, 0, lb_all[l], params)
        past = (cache_cmp_kv[l][page_table].reshape(dec_b, past_len, 2, NSA_GROUPS, NSA_HD),
                cache_sel_kv[l][page_table].reshape(dec_b, past_len, 2, NSA_GROUPS, NSA_HD),
                state_win_kv[l], state_hgrn[l], state_conv[l])
        y_s, st_s = decoder_layer(y_s, past, past_len, lb_all[l], params)
        new_p.append(st_p)
        new_s.append(st_s)

    def stack(group, i):
        return jnp.stack([st[i] for st in group], axis=0)

    return (y_p, y_s, stack(new_p, 0), stack(new_s, 0), stack(new_p, 1), stack(new_s, 1), stack(new_p, 2), stack(new_s, 2), stack(new_p, 3), stack(new_s, 3), stack(new_p, 4), stack(new_s, 4))


_drawn_inputs = setup_inputs


def setup_inputs(seed=0):
    import zlib

    import numpy as np

    out = dict(_drawn_inputs(seed))
    spreads = {}
    factors = {'hg_norm_w': 3.895,
     'ln_mix_post': 3.468,
     'ln_ffn_pre': 2.875,
     'ln_ffn_post': 17.646,
     'conv_b': 6.83,
     'cmp_pe': 3.201}
    for name, (base, spread) in spreads.items():
        noise = np.random.default_rng([zlib.crc32(name.encode()), seed]).standard_normal(out[name].shape)
        drawn = base * np.exp(spread * noise) if base else spread * noise
        out[name] = __import__('jax').numpy.asarray(drawn.astype(out[name].dtype))
    for name, factor in factors.items():
        out[name] = (out[name] * factor).astype(out[name].dtype)
    return out
```

```python
from contextlib import ExitStack, contextmanager

import concourse.bass as bass
from concourse import mybir

F32 = mybir.dt.float32
F32R = mybir.dt.float32r
I32 = mybir.dt.int32
U32 = mybir.dt.uint32
ALU = mybir.AluOpType
ACT = mybir.ActivationFunctionType
X = mybir.AxisListType.X
ds = bass.ds

P = 128
D = 2048
KT = D // P
SEQ, DB, DS = 256, 8, 8
SMP = DB * DS
T = SEQ + SMP
PAST, PAGE = 256, 128
N_PHYS = 20
HEADS, GROUPS, HPG = 8, 2, 4
BLK = 64
NBLK = PAST // BLK
NSEQ = 1 + DB
NCMP = GROUPS * NSEQ * NBLK
DFF = 5632
FT = DFF // P
UW = 2 + SEQ + DB * (DS + 2)
EPS = 1e-6
NEG = -1e30
SCALE = P ** -0.5
HC = 16
COL_KV, COL_GATE = 1024, 2560
COL_HQ, COL_HF, COL_HI, COL_HO, COL_MRG = 2584, 3608, 4632, 5656, 6680

N_A = 20
N_GATE = N_A
N_CMP = N_GATE + 1
N_HG = N_CMP + 8
N_MRG = N_HG + 4 * HEADS
N_OUT = N_MRG + 3 * KT
N_FFN = N_OUT + KT
PARTS = [16, 16, 12]
N_ALL = N_FFN + sum(2 * n + KT for n in PARTS)
R_HG, R_OUT, R_FFN = N_A, N_A + 4 * HEADS, N_A + 4 * HEADS + KT

BR = (1, 2, 0)


def columns(*parts):
    at, out = 0, {}
    for name, n in parts:
        out[name] = slice(at, at + n)
        at += n
    return out, at


CP, CP_N = columns(("ident", P), ("mean_d", P), ("mean_h", P), ("seg", T), ("causal_p", P), ("causal_s", SMP),
                   ("chunk_p", 8), ("chunk_s", 8))
CA, CA_N = columns(("bias_p", HEADS * 2 * P), ("bias_pc", 2 * HEADS * NCMP), ("bias_s", 4 * T), ("bias_sc", 4 * NCMP),
                   ("pick", 2 * P), ("head", 12), ("valid", 6))
PR, PR_N = columns(("ln", 4 * KT), ("lb", 16), ("hgn", 1), ("conv", 4 * 2 * FT))


class Count:

    def __init__(self, eng, sem):
        self.eng, self.sem, self.n, self.local = eng, sem, 0, 0

    def add(self, ins):
        ins.then_inc(self.sem, 1)
        self.n = self.n + 1
        self.local += 1

    def sync(self):
        self.eng.wait_ge(self.sem, self.n)

    @contextmanager
    def loop(self, times, per):
        start = self.n
        with self.eng.Fori(0, times) as i:
            self.n, self.local = i * per + start, 0
            yield i
            assert self.local == per, f"a turn counts {self.local}, not {per}"
        self.n = start + times * per


def turns(eng, times, turn, count=None):
    start = count.n if count else 0
    turn(0)
    per = count.n - start if count else 0
    with eng.Fori(1, times) as j:
        if count:
            count.n = j * per + start
        turn(j)
    if count:
        count.n = start + times * per


def later(n):
    return not (isinstance(n, int) and n == 0)


def layer(nc, a, o, xt_dram):
    BASE, LIMIT = 16512, 229344
    slab = nc.alloc_sbuf_tensor("slab", [P, LIMIT - BASE], mybir.dt.uint8)

    class Region:
        def __init__(self, at, limit=LIMIT - BASE):
            self.at, self.limit = at, limit

        def __call__(self, name, shape, dt=F32):
            size = 4
            for s in shape[1:]:
                size *= s
            where = self.at
            self.at += (size + 31) // 32 * 32
            assert self.at <= self.limit, (name, self.at - self.limit)
            return nc.alloc_sbuf_tensor_at(name, shape, dt, offset=BASE + where)

    pers = Region(0)
    cst = pers("cst", [P, CP_N])
    prm = pers("prm", [P, PR_N])
    lbx = pers("lbx", [P, 6, 8])
    ckT = pers("ckT", [P, NCMP])
    cv = pers("cv", [P, P])
    hid = pers("hid", [P, 2, NCMP])
    gates = pers("gates", [P, 3, 24])
    gate_p = pers("gate_p", [P, 2, 24])
    gate_s = pers("gate_s", [P, 4, 3])
    gtmp = pers("gtmp", [P, 4, 12])
    stat = pers("stat", [P, 8])
    sums = pers("sums", [P, 2, 4])
    nmax = pers("nmax", [P, 2, 4])
    wgt = pers("wgt", [P, 2, 4])
    ptab = pers("ptab", [P, 16], I32)
    ring = Region(pers.at)
    raw = ring("raw", [P, 2, 16, P])
    whi = ring("whi", [P, 2, 16, P], F32R)
    wlo = ring("wlo", [P, 2, 16, P], F32R)
    H = Region(ring.at)
    h_at = ring.at
    hH = H("hH", [P, KT, T], F32R)
    hL = H("hL", [P, KT, T], F32R)
    O = Region(H.at)
    o_at = H.at
    oH = O("oH", [P, KT, T], F32R)
    oL = O("oL", [P, KT, T], F32R)
    s_at = O.at

    r = Region(s_at)
    xtok = r("xtok", [P, 3, D])
    xT0 = r("xT0", [P, KT, T])
    hf = r("hf", [P, KT, T])
    r = Region(o_at, s_at)
    junk = r("junk", [P, D])
    rows = r("rows", [P, P])
    crow = r("crow", [2 * FT, 4, P])
    rsb0 = r("rsb0", [P, T])
    r = Region(s_at)
    cat = r("cat", [P, CA_N])
    kvq_at = r.at
    kvq = r("kvq", [P, N_A, T])
    kvtok = r("kvtok", [P, 3, 12 * P])
    late_at = r.at
    KTs = r("KTs", [P, 8, P])
    prob = r("prob", [P, 2 * (512 + NCMP)])
    r = Region(late_at)
    page = r("page", [P, 4, 512])
    w2 = r("w2", [P, 2, P])
    r = Region(o_at, s_at)
    kcT = r("kcT", [P, 4, NSEQ, PAST])
    pe4 = r("pe4", [P, 4, P])
    hsg = r("hsg", [P, 2, NCMP])
    pe_row = r("pe_row", [BLK, 2, P])
    half = 8 * T * 4
    r = Region(o_at + half, o_at + 2 * half)
    kv_sel = r("kv_sel", [P, 4, 4, P])
    pT0 = r("pT0", [P, 4, P])
    r = Region(o_at + 3 * half, o_at + 4 * half)
    kv_win = r("kv_win", [P, 4, 4, P])
    pT1 = r("pT1", [P, 4, P])
    pT = [pT0, pT1]
    r = Region(kvq_at, kvq_at + 4 * T * 4)
    pTs = r("pTs", [P, 7, P])
    qst = r("qst", [P, SEQ])
    r = Region(kvq_at + 6 * T * 4, kvq_at + 8 * T * 4)
    pTc = r("pTc", [P, 2, P])
    qs = Region(kvq_at + 10 * T * 4, kvq_at + 12 * T * 4)("qs", [P, 4, P])
    r = Region(s_at)
    kinv = r("kinv", [P, 2, T])
    kend = r("kend", [P, 2, T])
    qdec = r("qdec", [P, 2, T])
    ogs = r("ogs", [P, 2, T])
    cum = r("cum", [P, 2, T])
    vT = r("vT", [P, 2, T])
    fsig = r("fsig", [P, T])
    nsig = r("nsig", [P, T])
    fmul = r("fmul", [P, T])
    fset = r("fset", [P, T])
    osig = r("osig", [P, T])
    kend_tok = r("kend_tok", [P, 3, P])
    v_tok = r("v_tok", [P, 3, P])
    vmask = r("vmask", [P, 3, 8, P])
    att = r("att", [P, T])
    st = r("st", [P, 16, P])
    sfin = r("sfin", [P, 2, P])
    s0 = r("s0", [P, 2, DB, P])
    sn = r("sn", [P, 2, DB, P])
    osb = r("osb", [P, T])
    osq = r("osq", [P, T])
    orn = r("orn", [P, T])
    r = Region(s_at)
    mH = r("mH", [P, KT, T], F32R)
    mL = r("mL", [P, KT, T], F32R)
    ffn_at = r.at
    sga = r("sga", [P, 2, T])
    sgb = r("sgb", [P, 2, T])
    mix = r("mix", [P, 2, T])
    mix2 = r("mix2", [P, 2, T])
    r = Region(ffn_at)
    y1 = r("y1", [P, KT, T])
    hist = r("hist", [P, 2 * FT, 2 * DB])
    sq = r("sq", [P, 2, T])
    sqs = r("sqs", [P, T])
    rsb = r("rsb", [P, T])
    x1 = Region(o_at)("x1", [P, KT, T])
    acc = Region(o_at + KT * T * 4)("acc", [P, KT, T])
    hrow = Region(o_at + KT * T * 4)("hrow", [2 * FT, 2 * DB, P])
    r = Region(s_at)
    aH = r("aH", [P, KT, T], F32R)
    aL = r("aL", [P, KT, T], F32R)
    ue = r("ue", [P, 2, 2, UW])
    cc = r("cc", [P, 2, UW - 2])
    gg = r("gg", [P, T])
    newc = r("newc", [P, 2 * FT, 2 * NSEQ])
    assert r.at <= ffn_at + KT * T * 4
    r = Region(h_at, o_at)
    ytok = r("ytok", [P, 3, D])
    crow_out = r("crow_out", [2 * FT, 2 * NSEQ, P])

    ps = nc.alloc_psum_tensor("ps", [P, 8, 512], F32)

    def c_(name):
        return cst[:, CP[name]]

    ident = c_("ident")
    cat_ = {k: cat[:, v] for k, v in CA.items()}
    bias_p = cat_["bias_p"].rearrange("p (h k) -> p h k", h=HEADS)
    bias_pc = cat_["bias_pc"].rearrange("p (t h k) -> p t h k", t=2, h=HEADS)
    bias_s = cat_["bias_s"].rearrange("p (t k) -> p t k", t=4)
    bias_sc = cat_["bias_sc"].rearrange("p (t k) -> p t k", t=4)
    pick = cat_["pick"].rearrange("p (t k) -> p t k", t=2)
    ln = prm[:, PR["ln"]].rearrange("p (n k) -> p n k", n=4)
    conv = prm[:, PR["conv"]].rearrange("p (n k) -> p n k", n=4)
    hgn = prm[:, PR["hgn"]]

    S = nc.alloc_semaphore
    x_in, cst_in, rows_in, cat_in, w2_in, hrow_in, x1_in, xt_out = map(
        S, ("x_in", "cst_in", "rows_in", "cat_in", "w2_in", "hrow_in", "x1_in", "xt_out"))
    loaded = [S("loaded0"), S("loaded1")]
    ab_loaded = S("ab_loaded")
    hi_ready, lo_ready = S("hi_ready"), S("lo_ready")
    used = S("used")
    free = [S("free0"), S("free1")]
    dv_c, ac_c, po_c = S("dv_c"), S("ac_c"), S("po_c")
    par_ps, par_ok, ssq_ok, rms_v, rs_ok, rsb_ps, rsb_ok = map(
        S, ("par_ps", "par_ok", "ssq_ok", "rms_v", "rs_ok", "rsb_ps", "rsb_ok"))
    xt_ps, xt_ok, hf_ok, hh_ok, hl_ok = map(S, ("xt_ps", "xt_ok", "hf_ok", "hh_ok", "hl_ok"))
    tok_ps, tok_ok, kv_out = S("tok_ps"), S("tok_ok"), S("kv_out")
    ptab_in = S("ptab_in")
    page_in = [S(f"page_in{i}") for i in range(4)]
    pe_ps, pe_ok, page_ps, page_ok = S("pe_ps"), S("pe_ok"), S("page_ps"), S("page_ok")
    hid_sg, hid_ok, cc_ps, cc_ok = S("hid_sg"), S("hid_ok"), S("cc_ps"), S("cc_ok")
    gate_ok, gsel_ps, gsel_ok = S("gate_ok"), S("gsel_ps"), S("gsel_ok")
    q_ok, sc_ps, sc_rd, nm_ok, ex_ok, pn_ok = (S(n) for n in ("q_ok", "sc_ps", "sc_rd", "nm_ok", "ex_ok", "pn_ok"))
    pt_ps, pt_ok, ov_ps, oh_ok, ol_ok = (S(n) for n in ("pt_ps", "pt_ok", "ov_ps", "oh_ok", "ol_ok"))
    sel_in, win_in = S("sel_in"), S("win_in")
    kt_ps, kt_ok, ks_ps = S("kt_ps"), S("kt_ok"), S("ks_ps")
    f_sig, v_ok, q_rd, o_sig, f_done, og_ok = (S(n) for n in ("f_sig", "v_ok", "q_rd", "o_sig", "f_done", "og_ok"))
    t_ps, t_ok, m_ok, u_ps, s_ok, ho_ps, ho_sb, hm_ps, hv_ok, hr_ok, hn_ok, hoh, hol = (
        S(n) for n in ("t_ps", "t_ok", "m_ok", "u_ps", "s_ok", "ho_ps", "ho_sb", "hm_ps", "hv_ok", "hr_ok", "hn_ok",
                       "hoh", "hol"))
    s0_in = [S("s0_in0"), S("s0_in1")]
    st_out = [S("st_out0"), S("st_out1")]
    stat_zero, hist_ps, hist_ok = S("stat_zero"), S("hist_ps"), S("hist_ok")
    mg_rd = [S("mg_rd0"), S("mg_rd1")]
    mg_a, mg_mix, mg_hi, mg_lo = S("mg_a"), S("mg_mix"), S("mg_hi"), S("mg_lo")
    y_sq, y_add, mean_ps, mean_v, rstd_ok = S("y_sq"), S("y_add"), S("mean_ps"), S("mean_v"), S("rstd_ok")
    x_new, x_sq, x_add, h_new = S("x_new"), S("x_sq"), S("x_add"), S("h_new")
    h2h, h2l = S("h2h"), S("h2l")
    u_hist, u_ev, c_ok, g_ok, m_new, a_hi, a_lo, newc_ok = (
        S(n) for n in ("u_hist", "u_ev", "c_ok", "g_ok", "m_new", "a_hi", "a_lo", "newc_ok"))
    d_acc, d_sq, d_add = S("d_acc"), S("d_sq"), S("d_add")
    y_fin, yt_ps, yt_ok, nc_ps, nc_ok, y_out, copy_out = (
        S(n) for n in ("y_fin", "yt_ps", "yt_ok", "nc_ps", "nc_ok", "y_out", "copy_out"))

    w_in = a["w_in"][0]
    HGCOL = [COL_HF, COL_HI, COL_HQ, COL_HO]

    def tile_src(w, rows, at, step=0):
        if isinstance(step, int):
            return w[rows, at + step:at + step + P].rearrange("(k p) n -> p k n", p=P)
        return w[rows, at:][:, ds(step, P)].rearrange("(k p) n -> p k n", p=P)

    block = ctx_block = nc.Block()
    with block:
        @block.sync
        def _(sp):
            sp.dma_start(xtok[:, 0, :], a["x_prompt"][0, 0:P, :]).then_inc(x_in, 16)
            sp.dma_start(xtok[:, 1, :], a["x_prompt"][0, P:SEQ, :]).then_inc(x_in, 16)
            sp.dma_start(xtok[0:SMP, 2, :], a["x_sample"].rearrange("b s d -> (b s) d")).then_inc(x_in, 16)

            def load(n, slot, src, k0=0, kn=16, first=False, direct=False, sem=None):
                if not first:
                    sp.wait_ge(lo_ready, n - 1)
                    if direct:
                        sp.wait_ge(used, n - 1)
                sp.dma_start(raw[:, slot, k0:k0 + kn, :], src).then_inc(sem or loaded[slot], 16)

            for u in range(2):
                load(u, u, tile_src(w_in, slice(0, D), COL_KV + u * P), first=True)
            with sp.Fori(0, 5) as j:
                for u in range(2):
                    load(j * 2 + (2 + u), u, tile_src(w_in, slice(0, D), COL_KV + (2 + u) * P, j * 256))
            with sp.Fori(0, 4) as j:
                for u in range(2):
                    load(j * 2 + (12 + u), u, tile_src(w_in, slice(0, D), u * P, j * 256))
            load(N_GATE, N_GATE % 2, tile_src(w_in, slice(0, D), COL_GATE))
            for c in range(2):
                for q in range(4):
                    n = N_CMP + 4 * c + q
                    load(n, n % 2, a["cmp_w1"][0, 16 * q:16 * q + 16, c].rearrange("l d e -> d l e"), direct=True)
            for h in range(1):
                for u in range(4):
                    n = N_HG + u
                    load(n, n % 2, tile_src(w_in, slice(0, D), HGCOL[u]), direct=True)
            with sp.Fori(0, HEADS - 1) as h:
                for u in range(4):
                    load(h * 4 + (N_HG + 4 + u), (N_HG + u) % 2, tile_src(w_in, slice(0, D), HGCOL[u] + P, h * P))
            def branch_src(name, m):
                return a[name][0].rearrange("(k p) (m n) -> m p k n", p=P, n=P)[ds(m, 1)].rearrange(
                    "o p k n -> (o p) k n")

            with sp.Fori(0, KT // 2) as j:
                for v in range(2):
                    for u in range(3):
                        n, slot = j * 6 + (N_MRG + 3 * v + u), (N_MRG + 3 * v + u) % 2
                        if u < 2:
                            load(n, slot, tile_src(w_in, slice(0, D), COL_MRG + u * D + v * P, j * 256))
                        else:
                            load(n, slot, branch_src("w_branch_a", j * 2 + v), kn=8)
                            sp.dma_start(raw[:, slot, 8:16, :],
                                         branch_src("w_branch_b", j * 2 + v)
                                         ).then_inc(ab_loaded, 16)
            with sp.Fori(0, KT // 2) as j:
                for u in range(2):
                    load(j * 2 + (N_OUT + u), (N_OUT + u) % 2,
                         tile_src(a["w_out"][0], slice(0, D), u * P, j * 256))
            n0, t0 = N_FFN, 0
            for cnt in PARTS:
                with sp.Fori(0, cnt) as i:
                    for u in range(2):
                        load(i * 2 + (n0 + u), (n0 + u) % 2,
                             tile_src(a["w_up"][0], slice(0, D), u * DFF + t0 * P, i * P))
                n0 += 2 * cnt
                with sp.Fori(0, KT // 2) as j:
                    for u in range(2):
                        load(j * 2 + (n0 + u), (n0 + u) % 2,
                             tile_src(a["w_down"][0], slice(t0 * P, (t0 + cnt) * P), u * P, j * 256), kn=cnt)
                n0 += KT
                t0 += cnt

        @block.gpsimd
        def _(po):
            po.dma_start(ptab[0:1, :], a["page_table"].rearrange("(o b) n -> o (b n)", o=1)).then_inc(ptab_in, 16)
            po.dma_start(pe_row[:], a["cmp_pe"][0]).then_inc(w2_in, 16)
            po.wait_ge(x_in, 48)
            po.wait_ge(xt_ok, KT)
            po.dma_start(xt_dram.rearrange("p (k t) -> p k t", k=KT), xT0[:]).then_inc(xt_out, 16)
            win = a["state_win_kv"][0].rearrange("b w c g d -> b (w c g d)")
            po.dma_start(o[7][0].rearrange("b w c g d -> b (w c g d)")[:, 0:(PAST - DS) * 512],
                         win[:, DS * 512:PAST * 512]).then_inc(copy_out, 16)
            po.wait_ge(ptab_in, 16)
            po.wait_ge(hh_ok, KT)
            po.wait_ge(hl_ok, KT)
            po.dma_start(cat[:], a["att_const"]).then_inc(cat_in, 16)
            po.dma_start(w2[:], a["cmp_w2"][0].rearrange("c e f -> e c f")).then_inc(w2_in, 16)
            cmp_pages = a["cache_cmp_kv"][0].rearrange("n t c g d -> n t (c g d)")
            sel_pages = a["cache_sel_kv"][0]

            def cmp_page(i, slot):
                idx = po.value_load(ptab[0:1, ds(i, 1)] if not isinstance(i, int) else ptab[0:1, i:i + 1],
                                    min_val=0, max_val=N_PHYS - 1)
                po.dma_start(page[:, slot, :], cmp_pages[ds(idx, 1)].rearrange("o t c -> (o t) c")
                             ).then_inc(page_in[slot], 16)

            for i in range(4):
                cmp_page(i, i)
            with po.Fori(0, 3) as j:
                for u in range(4):
                    po.wait_ge(page_ps, j * 4 + (u + 1))
                    cmp_page(j * 4 + (4 + u), u)
            po.wait_ge(tok_ok, 12)
            for n, name in enumerate((2, 4, 6)):
                cols = slice(512 * n, 512 * n + 512)
                po.dma_start(o[name][0, 0].rearrange("(a p) c g d -> p a (c g d)", p=P),
                             kvtok[:, 0:2, cols]).then_inc(kv_out, 16)
            for n, name in enumerate((3, 5)):
                po.dma_start(o[name][0].rearrange("b s c g d -> (b s) (c g d)"),
                             kvtok[0:SMP, 2, 512 * n:512 * n + 512]).then_inc(kv_out, 16)
            for b in range(DB):
                po.dma_start(o[7][0, b, PAST - DS:PAST].rearrange("s c g d -> s (c g d)"),
                             kvtok[b * DS:b * DS + DS, 2, 1024:1536]).then_inc(kv_out, 16)
            po.wait_ge(hid_ok, 2)
            for k in range(4):
                g, bh = k // 2, k % 2
                if k:
                    po.wait_ge(ov_ps, 16 + k)
                for j in range(4):
                    for t in range(2):
                        i = (4 * bh + j) * 2 + t
                        idx = po.value_load(ptab[0:1, i:i + 1], min_val=0, max_val=N_PHYS - 1)
                        po.dma_start(kv_sel[:, j, 2 * t:2 * t + 2, :],
                                     sel_pages[ds(idx, 1), :, :, g, :].rearrange("o t c d -> (o t) c d")
                                     ).then_inc(sel_in, 16)
                for j in range(4):
                    for t in range(2):
                        po.dma_start(kv_win[:, j, 2 * t:2 * t + 2, :],
                                     a["state_win_kv"][0, 4 * bh + j, t * PAGE:(t + 1) * PAGE, :, g, :]
                                     ).then_inc(win_in, 16)
            po.wait_ge(ol_ok, 20)
            st_in = a["state_hgrn"][0].rearrange("b h k v -> h k b v")
            sp_out = o[8][0, 0]
            ss_out = o[9][0].rearrange("b h k v -> h k b v")

            def state_in(h, par):
                src = st_in[ds(h, 1)].rearrange("o k b v -> (o k) b v")
                po.dma_start(s0[:, par], src).then_inc(s0_in[par], 16)

            def state_out(h, par):
                po.wait_ge(s_ok, h + 1)
                po.dma_start(sp_out[ds(h, 1)].rearrange("o k v -> (o k) v"), sfin[:, par]).then_inc(st_out[par], 16)
                po.dma_start(ss_out[ds(h, 1)].rearrange("o k b v -> (o k) b v"), sn[:, par]).then_inc(st_out[par], 16)

            state_in(0, 0)
            state_in(1, 1)
            with po.Fori(0, HEADS // 2 - 1) as j:
                for par in range(2):
                    state_out(j * 2 + par, par)
                    po.wait_ge(ho_ps, j * 2 + (par + 1))
                    state_in(j * 2 + (par + 2), par)
            for par in range(2):
                state_out(HEADS - 2 + par, par)
            po.wait_ge(mg_lo, KT)
            po.wait_ge(used, N_OUT)
            po.wait_ge(xt_out, 16)
            po.dma_start(x1[:], xt_dram.rearrange("p (k t) -> p k t", k=KT)).then_inc(x1_in, 16)
            po.dma_start(hrow[:], a["state_conv"][0].rearrange("b j (f p) -> f (b j) p", p=P)).then_inc(hrow_in, 16)
            po.wait_ge(nc_ok, 5)
            po.dma_start(o[10][0, 0].rearrange("j (f p) -> f j p", p=P), crow_out[:, 0:2, :]).then_inc(y_out, 16)
            po.dma_start(o[11][0].rearrange("b j (f p) -> f (b j) p", p=P), crow_out[:, 2:, :]).then_inc(y_out, 16)
            for q in range(4):
                po.wait_ge(yt_ok, 4 * q + 4)
                cols = slice(512 * q, 512 * q + 512)
                po.dma_start(o[0][0].rearrange("(a p) d -> p a d", p=P)[:, :, cols], ytok[:, 0:2, cols]
                             ).then_inc(y_out, 16)
                po.dma_start(o[1].rearrange("b s d -> (b s) d")[:, cols], ytok[0:SMP, 2, cols]).then_inc(y_out, 16)
            po.wait_ge(copy_out, 16)
            po.wait_ge(kv_out, 16 * 13)
            for par in range(2):
                po.wait_ge(st_out[par], 16 * HEADS)
            po.wait_ge(y_out, 16 * 10)

        @block.scalar
        def _(act):
            A = Count(act, ac_c)

            def split(n, half, slot, ab=None):
                act.wait_ge(loaded[slot], half * 16 + 16)
                if ab is not None:
                    act.wait_ge(ab_loaded, ab * 16 + 16)
                if not isinstance(n, int) or n >= 2:
                    act.wait_ge(used, n - 1)
                act.activation(whi[:, slot], raw[:, slot], ACT.Copy).then_inc(hi_ready, 1)

            def split_after(n, i=None, per=0):
                if n + 2 < N_ALL:
                    m = n + 2
                    if i is None:
                        split(m, m // 2, m % 2)
                    else:
                        split(i * per + m, i * (per // 2) + m // 2, m % 2)

            act.dma_start(cst[:], a["const"]).then_inc(cst_in, 16)
            for n, name in enumerate(("ln_mix_pre", "ln_mix_post", "ln_ffn_pre", "ln_ffn_post")):
                act.dma_start(rows[KT * n:KT * n + KT, :], a[name][0].rearrange("(k p) -> k p", p=P)
                              ).then_inc(rows_in, 16)
            act.dma_start(rows[64:80, :], a["hg_lb_raw"].rearrange("r (k p) -> (r k) p", p=P)).then_inc(rows_in, 16)
            act.dma_start(rows[80:81, :], a["hg_norm_w"]).then_inc(rows_in, 16)
            act.dma_start(crow[:, 0:3, :], a["conv_w"][0].rearrange("j (f p) -> f j p", p=P)).then_inc(rows_in, 16)
            act.dma_start(crow[:, 3, :], a["conv_b"][0].rearrange("(f p) -> f p", p=P)).then_inc(rows_in, 16)
            act.wait_ge(x_in, 48)
            act.wait_ge(stat_zero, 1)
            for i in range(3):
                m = P if i < 2 else SMP
                if i:
                    A.sync()
                ins = act.activation(junk[0:m, :], xtok[0:m, i, :], ACT.Square, accum_out=stat[0:m, i:i + 1])
                if i < 2:
                    A.add(ins)
                else:
                    ins.then_inc(ssq_ok, 1)
            act.wait_ge(rms_v, 1)
            act.activation(stat[:, 3:6], stat[:, 3:6], ACT.Sqrt).then_inc(rs_ok, 1)
            for k in range(KT):
                act.wait_ge(xt_ps, k + 1)
                act.activation(xT0[:, k, :], ps[:, 2 + k % 6, 0:T], ACT.Copy).then_inc(xt_ok, 1)
            act.wait_ge(par_ps, 1)
            act.activation(prm[:], ps[:, 1, 0:PR_N], ACT.Copy).then_inc(par_ok, 1)
            act.wait_ge(rsb_ps, 1)
            act.activation(rsb0[:], ps[:, 0, 0:T], ACT.Copy).then_inc(rsb_ok, 1)
            act.wait_ge(rms_v, 2)
            act.activation(lbx[:, 2:4, :], lbx[:, 0:2, :], ACT.Exp).then_inc(rs_ok, 1)
            split(0, 0, 0)
            split(1, 0, 1)
            for k in range(KT):
                act.wait_ge(hf_ok, k + 1)
                act.activation(hH[:, k, :], hf[:, k, :], ACT.Copy).then_inc(hh_ok, 1)
            act.wait_ge(xt_out, 16)
            def turn(j):
                for u in range(2):
                    split_after(u, j, 2)
                    act.wait_ge(used, j * 2 + (u + 1))
                    act.activation(kvq[:, ds(j * 2 + u, 1), :], ps[:, u:u + 1, 0:T], ACT.Copy).then_inc(free[u], 1)

            turns(act, N_A//2, turn)
            split_after(N_GATE)
            act.wait_ge(used, N_GATE + 1)
            act.activation(gates[:], ps[:, 2, 0:72].rearrange("p (a b) -> p a b", a=3), ACT.Sigmoid
                           ).then_inc(gate_ok, 1)
            act.wait_ge(pe_ps, 1)
            for r_ in range(2):
                for g in range(2):
                    ins = act.activation(pe4[:].rearrange("p (c g) (r l) -> p c g r l", c=2, r=2)[:, :, g, r_, :],
                                         ps[:, 4, 0:P].rearrange("p (c l) -> p c l", c=2), ACT.Copy)
                    if (r_, g) == (1, 1):
                        ins.then_inc(pe_ok, 1)
            for f in range(12):
                act.wait_ge(tok_ps, f + 1)
                A.add(act.activation(kvtok[:, 0:2, f * P:f * P + P],
                                     ps[:, f % 2, 0:256].rearrange("p (a d) -> p a d", a=2), ACT.Copy))
                act.activation(kvtok[0:SMP, 2, f * P:f * P + P], ps[0:SMP, f % 2, 256:384], ACT.Copy
                               ).then_inc(tok_ok, 1)
            for c in range(2):
                for q in range(4):
                    split_after(N_CMP + 4 * c + q)
                act.wait_ge(used, N_CMP + 4 * c + 4)
                act.activation(hsg[:, c, :], ps[:, c, 0:NCMP], ACT.Sigmoid).then_inc(hid_sg, 1)
            act.wait_ge(cc_ps, 1)
            act.activation(ckT[:], ps[:, 2, 0:NCMP], ACT.Copy).then_inc(cc_ok, 1)
            act.activation(cv[0:NCMP, :], ps[0:NCMP, 3, 0:P], ACT.Copy).then_inc(cc_ok, 1)

            def exps(u, par, nk, width):
                act.wait_ge(nm_ok, u + 1)
                for b in range(3):
                    w = slice(b * width, b * width + nk) if b < 2 else slice(2 * width, 2 * width + NCMP)
                    base = par
                    ins = act.activation(prob[:, base + w.start:base + w.stop], prob[:, base + w.start:base + w.stop],
                                         ACT.Exp, bias=nmax[:, (1 if base else 0), BR[b]:BR[b] + 1],
                                         accum_out=sums[:, (1 if base else 0), BR[b]:BR[b] + 1])
                    if b == 2:
                        ins.then_inc(ex_ok, 1)
                    else:
                        A.add(ins)

            PW = 512 + NCMP
            for g in range(GROUPS):
                def turn(hh):
                    u0 = hh * 2 + 8 * g
                    if later(u0):
                        act.wait_ge(sc_ps, u0)
                    act.activation(qst[:], kvq[:, ds(hh + (12 + 4 * g), 1), 0:SEQ].rearrange("p o t -> p (o t)"),
                                   ACT.Copy, scale=SCALE).then_inc(q_ok, 1)
                    for qt in range(2):
                        exps(u0 + qt, qt * PW, (qt + 1) * P, (qt + 1) * P)
                    for qt in range(2):
                        u = u0 + qt
                        act.wait_ge(pt_ps, u + 1)
                        if later(u):
                            act.wait_ge(ov_ps, u)
                        A.add(act.activation(pT[qt][:, 0:2 * (qt + 1), :],
                                             ps[:, 6, 0:256 * (qt + 1)].rearrange("p (a d) -> p a d", d=P), ACT.Copy))
                        act.activation(pTc[0:NCMP, qt, :], ps[0:NCMP, 7, 0:P], ACT.Copy).then_inc(pt_ok, 1)
                        act.wait_ge(ov_ps, u + 1)
                        act.activation(oH[:, ds(hh + 4 * g, 1), qt * P:qt * P + P], ps[:, qt:qt + 1, 0:P], ACT.Copy
                                       ).then_inc(oh_ok, 1)

                turns(act, HPG, turn, A)
            for k in range(4):
                g, bh = k // 2, k % 2
                for h4 in range(4):
                    ins = act.activation(
                        qs[:, k, :].rearrange("p (j h s) -> p j h s", j=4, h=4)[:, :, h4, :],
                        kvq[:, 12 + 4 * g + h4, SEQ + 32 * bh:SEQ + 32 * bh + 32].rearrange("p (j s) -> p j s", j=4),
                        ACT.Copy, scale=SCALE)
                ins.then_inc(q_ok, 1)
            for k in range(4):
                g, bh = k // 2, k % 2
                u = 16 + k
                for br in range(2):
                    act.wait_ge(kt_ps, 2 * k + br + 1)
                    if br or k:
                        act.wait_ge(ks_ps, 2 * k + br)
                    A.add(act.activation(KTs[:, 0:4, :], ps[:, 5, :].rearrange("p (a d) -> p a d", a=4), ACT.Copy))
                    act.activation(KTs[:, 4:8, :], ps[:, 6, :].rearrange("p (a d) -> p a d", a=4), ACT.Copy
                                   ).then_inc(kt_ok, 1)
                exps(u, 0, T, T)
                act.wait_ge(pt_ps, u + 1)
                A.add(act.activation(pTs[:, 0:2, :], ps[:, 5, 0:256].rearrange("p (a d) -> p a d", a=2), ACT.Copy))
                A.add(act.activation(pTs[0:SMP, 2, :], ps[0:SMP, 5, 256:384], ACT.Copy))
                A.add(act.activation(pTs[:, 3:5, :], ps[:, 6, 0:256].rearrange("p (a d) -> p a d", a=2), ACT.Copy))
                A.add(act.activation(pTs[0:SMP, 5, :], ps[0:SMP, 6, 256:384], ACT.Copy))
                act.activation(pTs[0:NCMP, 6, :], ps[0:NCMP, 7, 0:P], ACT.Copy).then_inc(pt_ok, 1)
                act.wait_ge(ov_ps, u + 1)
                act.activation(
                    oH[:, 4 * g:4 * g + 4, SEQ + 32 * bh:SEQ + 32 * bh + 32].rearrange("p h (j s) -> p h j s", j=4),
                    ps[:, 0, 0:P].rearrange("p (j h s) -> p h j s", j=4, h=4), ACT.Copy).then_inc(oh_ok, 1)

            def tail1(h):
                act.wait_ge(t_ps, h + 1)
                A.add(act.activation(kend_tok[:, 0:2, :], ps[:, 2, 0:256].rearrange("p (a d) -> p a d", a=2), ACT.Copy))
                A.add(act.activation(kend_tok[0:SMP, 2, :], ps[0:SMP, 2, 256:384], ACT.Copy))
                A.add(act.activation(v_tok[:, 0:2, :], ps[:, 3, 0:256].rearrange("p (a d) -> p a d", a=2), ACT.Copy))
                act.activation(v_tok[0:SMP, 2, :], ps[0:SMP, 3, 256:384], ACT.Copy).then_inc(t_ok, 1)

            def tail2(h):
                act.wait_ge(ho_ps, h + 1)
                if later(h):
                    act.wait_ge(hol, h)
                A.add(act.activation(osq[:], ps[:, 5, 0:T], ACT.Square))
                act.activation(osb[:], ps[:, 5, 0:T], ACT.Copy).then_inc(ho_sb, 1)

            def tail3(h):
                act.wait_ge(hv_ok, h + 1)
                act.activation(orn[:], orn[:], ACT.Sqrt).then_inc(hr_ok, 1)
                act.wait_ge(hn_ok, h + 1)
                act.activation(oH[:, ds(h + 8, 1), :], osb[:].rearrange("p (o t) -> p o t", o=1), ACT.Copy
                               ).then_inc(hoh, 1)

            def window(h, par, i=None, k=0):
                n = N_HG + 4 * k
                nn = n if i is None else i * 8 + n
                if k:
                    tail1(h - 1)
                split_after(n, i, 8)
                act.wait_ge(used, nn + 1)
                if later(h):
                    act.wait_ge(f_done, h)
                A.add(act.activation(fsig[:], ps[:, 0, 0:T], ACT.Sigmoid))
                act.activation(nsig[:], ps[:, 0, 0:T], ACT.Sigmoid, scale=-1.0).then_inc(free[0], 1)
                split_after(n + 1, i, 8)
                act.wait_ge(used, nn + 2)
                act.activation(vT[:, par, :], ps[:, 1, 0:T], ACT.Copy).then_inc(free[1], 1)
                if k:
                    tail2(h - 1)
                split_after(n + 2, i, 8)
                if k:
                    tail3(h - 1)
                split_after(n + 3, i, 8)
                act.wait_ge(used, nn + 4)
                act.wait_ge(free[1], h * 2 + R_HG // 2)
                act.activation(osig[:], ps[:, 1, 0:T], ACT.Sigmoid).then_inc(o_sig, 1)

            act.wait_ge(kv_out, 16 * 13)
            act.wait_ge(ol_ok, 20)
            window(0, 0)
            window(1, 1, None, 1)
            window(2, 0, None, 2)
            with A.loop(2, 10) as i:
                window(i * 2 + 3, 1, i, 3)
                window(i * 2 + 4, 0, i, 4)
            window(7, 1, None, 7)
            tail1(7)
            tail2(7)
            tail3(7)

            act.wait_ge(hol, HEADS)
            for par in range(2):
                act.wait_ge(st_out[par], 16 * HEADS)
            def turn(j):
                for v in range(2):
                    m, n = j * 2 + v, N_MRG + 3 * v
                    for u in range(3):
                        c = n + u + 2
                        split(j * 6 + c, j * 3 + c // 2, c % 2, m if u == 0 else None)
                        act.wait_ge(used, j * 6 + (n + u + 1))
                        if u == 0:
                            if later(j):
                                act.wait_ge(mg_rd[v], j)
                            act.activation(sga[:, v, :], ps[:, 4 * v, 0:T], ACT.Sigmoid).then_inc(mg_a, 1)
                        elif u == 1:
                            act.activation(sgb[:, v, :], ps[:, 4 * v + 1, 0:T], ACT.Sigmoid).then_inc(mg_a, 1)
                        else:
                            act.wait_ge(mg_mix, m + 1)
                            act.activation(mH[:, ds(m, 1), :], mix[:, v:v + 1, :], ACT.Copy).then_inc(mg_hi, 1)

            turns(act, KT//2, turn)
            def turn(j):
                for u in range(2):
                    m = j * 2 + u
                    split_after(N_OUT + u, j, 2)
                    act.wait_ge(used, m + (N_OUT + 1))
                    if later(m):
                        act.wait_ge(y_add, m)
                    act.activation(sq[:, u, :], ps[:, u, 0:T], ACT.Square).then_inc(y_sq, 1)
                    act.activation(y1[:, ds(m, 1), :], ps[:, u:u + 1, 0:T], ACT.Copy).then_inc(free[u], 1)

            turns(act, KT//2, turn)
            for i in range(4):
                act.wait_ge(hist_ps, i + 1)
                act.activation(hist[:, :, 4 * i:4 * i + 4],
                               ps[:, 3 + i, 0:4 * 2 * FT].rearrange("p (b f) -> p f b", b=4), ACT.Copy
                               ).then_inc(hist_ok, 1)
            act.wait_ge(mean_v, 1)
            act.activation(rsb[:], rsb[:], ACT.Sqrt).then_inc(rstd_ok, 1)
            for k in range(KT):
                act.wait_ge(x_new, k + 1)
                if k >= 2:
                    act.wait_ge(x_add, k - 1)
                act.activation(sq[:, k % 2, :], x1[:, k, :], ACT.Square).then_inc(x_sq, 1)
            act.wait_ge(mean_v, 2)
            act.activation(rsb[:], rsb[:], ACT.Sqrt).then_inc(rstd_ok, 1)
            for k in range(KT):
                act.wait_ge(h_new, k + 1)
                act.activation(hH[:, k, :], y1[:, k, :], ACT.Copy).then_inc(h2h, 1)

            n0, r0, i0 = N_FFN, R_FFN, 0
            for part, cnt in enumerate(PARTS):
                def turn(j):
                    for par in range(2):
                        i = j * 2 + (i0 + par)
                        for s in range(2):
                            c = 2 * par + s
                            split_after(n0 + c, j, 4)
                            act.wait_ge(used, j * 4 + (n0 + c + 1))
                            act.wait_ge(u_hist, i * 2 + (s + 1))
                            A.add(act.activation(ue[:, par, s, 2:2 + SEQ], ps[:, s, 0:SEQ], ACT.Copy))
                            act.activation(ue[:, par, s, 2 + SEQ:UW].rearrange("p (b c) -> p b c", b=DB)[:, :, 2:],
                                           ps[:, s, SEQ:T].rearrange("p (b c) -> p b c", b=DB), ACT.Copy
                                           ).then_inc(free[s], 1)
                            A.sync()
                            act.wait_ge(free[s], j * 2 + (r0 // 2 + par + 1))
                            if later(i):
                                act.wait_ge(m_new, i)
                            col = i + s * FT
                            act.activation(cc[:, s, :], ue[:, par, s, 0:UW - 2], ACT.Identity,
                                           scale=conv[:, 0, ds(col, 1)], bias=conv[:, 3, ds(col, 1)]
                                           ).then_inc(u_ev, 1)
                        act.wait_ge(c_ok, i * 2 + 2)
                        act.activation(cc[:, 1, :], cc[:, 1, :], ACT.Gelu_apprx_tanh).then_inc(g_ok, 1)
                        act.wait_ge(m_new, i + 1)
                        act.activation(aH[:, ds(j * 2 + par, 1), :], gg[:].rearrange("p (o t) -> p o t", o=1), ACT.Copy
                                       ).then_inc(a_hi, 1)

                turns(act, cnt//2, turn, A)
                n0 += 2 * cnt
                r0 += 2 * cnt
                i0 += cnt
                if part < 2:
                    def turn(j):
                        for u in range(2):
                            split_after(n0 + u, j, 2)

                    turns(act, KT//2, turn)
                else:
                    for i in range(5):
                        w = 4 if i < 4 else 2
                        act.wait_ge(nc_ps, i + 1)
                        act.activation(crow_out[:, 4 * i:4 * i + w, :],
                                       ps[0:2 * FT, 3 + i, 0:w * P].rearrange("p (a d) -> p a d", a=w), ACT.Copy
                                       ).then_inc(nc_ok, 1)
                    act.wait_ge(x_add, KT)

                    def square(m, u, j):
                        act.wait_ge(free[u], j + (r0 // 2 + 1))
                        if later(m):
                            act.wait_ge(d_add, m)
                        act.activation(sq[:, u, :], acc[:, ds(m, 1), :].rearrange("p o t -> p (o t)"), ACT.Square
                                       ).then_inc(d_sq, 1)

                    def turn(j):
                        for u in range(2):
                            split_after(n0 + u, j, 2)
                            square(j * 2 + u, u, j)

                    turns(act, KT//2-1, turn)
                    for u in range(2):
                        square(KT - 2 + u, u, KT // 2 - 1)
                n0 += KT
                r0 += KT
            act.wait_ge(mean_v, 3)
            act.activation(rsb[:], rsb[:], ACT.Sqrt).then_inc(rstd_ok, 1)
            for k in range(KT):
                act.wait_ge(yt_ps, k + 1)
                b = 3 + k % 4
                A.add(act.activation(ytok[:, 0:2, k * P:k * P + P],
                                     ps[:, b, 0:256].rearrange("p (a d) -> p a d", a=2), ACT.Copy))
                act.activation(ytok[0:SMP, 2, k * P:k * P + P], ps[0:SMP, b, 256:384], ACT.Copy).then_inc(yt_ok, 1)

        @block.vector
        def _(dve):
            V = Count(dve, dv_c)
            TT, TS, STT = dve.tensor_tensor, dve.tensor_scalar, dve.scalar_tensor_tensor

            def split(n, slot):
                dve.wait_ge(hi_ready, n + 1)
                TT(wlo[:, slot], raw[:, slot], whi[:, slot].bitcast(F32), ALU.subtract).then_inc(lo_ready, 1)

            def split_after(n, i=None, per=0):
                if n + 2 < N_ALL:
                    split(n + 2 if i is None else i * per + (n + 2), n % 2)

            dve.memset(stat[:], 0.0).then_inc(stat_zero, 1)
            dve.wait_ge(stat_zero, 1)
            dve.wait_ge(ssq_ok, 1)
            V.add(TS(stat[:, 3:6], stat[:, 0:3], 1.0 / D, EPS, ALU.mult, ALU.add))
            V.sync()
            dve.reciprocal(stat[:, 3:6], stat[:, 3:6]).then_inc(rms_v, 1)
            dve.wait_ge(par_ok, 1)
            lb0, lb1 = prm[:, PR["lb"]][:, 0:8], prm[:, PR["lb"]][:, 8:16]
            V.add(TT(lbx[:, 4, :], lb0, lb1, ALU.max))
            V.sync()
            V.add(TT(lbx[:, 0, :], lb0, lbx[:, 4, :], ALU.subtract))
            TT(lbx[:, 1, :], lb1, lbx[:, 4, :], ALU.subtract).then_inc(rms_v, 1)
            dve.wait_ge(rsb_ok, 1)
            for k in range(KT):
                dve.wait_ge(xt_ok, k + 1)
                STT(hf[:, k, :], xT0[:, k, :], ln[:, 0, k:k + 1], rsb0[:], ALU.mult, ALU.mult).then_inc(hf_ok, 1)
            dve.wait_ge(rs_ok, 2)
            V.add(TT(lbx[:, 4, :], lbx[:, 2, :], lbx[:, 3, :], ALU.add))
            V.sync()
            V.add(dve.reciprocal(lbx[:, 5, :], lbx[:, 4, :]))
            V.sync()
            V.add(TT(lbx[:, 0, :], lbx[:, 2, :], lbx[:, 5, :], ALU.mult))
            V.sync()
            V.add(TS(lbx[:, 1, :], lbx[:, 0, :], -1.0, 1.0, ALU.mult, ALU.add))
            split(0, 0)
            split(1, 1)
            for k in range(KT):
                dve.wait_ge(hh_ok, k + 1)
                TT(hL[:, k, :], hf[:, k, :], hH[:, k, :].bitcast(F32), ALU.subtract).then_inc(hl_ok, 1)
            def turn(j):
                for u in range(2):
                    split_after(u, j, 2)

            turns(dve, N_A//2, turn)
            split_after(N_GATE)
            dve.wait_ge(pe_ok, 1)
            dve.wait_ge(free[0], N_A // 2)
            dve.wait_ge(free[1], N_A // 2)
            TT(kcT[:, :, 0, :].rearrange("p c (r t) -> p c r t", r=2),
               kvq[:, 0:4, 0:SEQ].rearrange("p c (r t) -> p c r t", r=2),
               pe4[:].unsqueeze(2).to_broadcast([P, 4, 2, P]), ALU.add).then_inc(page_ok, 1)
            def turn(j):
                for u in range(4):
                    dve.wait_ge(page_ps, j * 4 + (u + 1))
                    TT(kcT[:, :, ds(j * 2 + (1 + u // 2), 1), (u % 2) * P:(u % 2) * P + P],
                       ps[:, 4 + u, :].rearrange("p (c o t) -> p c o t", c=4, o=1),
                       pe4[:].unsqueeze(2), ALU.add).then_inc(page_ok, 1)

            turns(dve, DB//2, turn)
            dve.wait_ge(gate_ok, 1)
            dve.wait_ge(cat_in, 16)
            V.add(TT(gate_p[:].rearrange("p t (h r) -> p t h r", r=3),
                     gates[:, 0:2, :].rearrange("p t (h r) -> p t h r", r=3),
                     cat_["valid"].rearrange("p (t o r) -> p t o r", t=2, o=1).to_broadcast([P, 2, HEADS, 3]), ALU.mult))
            dve.wait_ge(gsel_ps, 1)
            for k in range(4):
                c0 = (k % 2) * 24 + (k // 2) * 12
                V.add(TT(gtmp[:, k, :], ps[:, 3, c0:c0 + 12], cat_["head"], ALU.mult))
            V.sync()
            dve.tensor_reduce(gate_s[:], gtmp[:].rearrange("p k (h r) -> p k r h", r=3), X, ALU.add).then_inc(gsel_ok, 1)
            for c in range(2):
                for q in range(4):
                    split_after(N_CMP + 4 * c + q)
                dve.wait_ge(hid_sg, c + 1)
                TT(hid[:, c, :], ps[:, c, 0:NCMP], hsg[:, c, :], ALU.mult).then_inc(hid_ok, 1)
            dve.wait_ge(gsel_ok, 1)

            PW = 512 + NCMP

            def scored(u, base, nk, src, bias, src_c, bias_c):
                row = 1 if base else 0
                dve.wait_ge(sc_ps, u + 1)
                V.add(TT(prob[:, base:base + 2 * nk].rearrange("p (b k) -> p b k", b=2), src, bias, ALU.add))
                TT(prob[:, base + 2 * nk:base + 2 * nk + NCMP], src_c, bias_c, ALU.add).then_inc(sc_rd, 1)
                V.sync()
                V.add(dve.tensor_reduce(nmax[:, row, 1:3],
                                        prob[:, base:base + 2 * nk].rearrange("p (b k) -> p b k", b=2), X, ALU.max,
                                        negate=True))
                dve.wait_ge(sc_rd, u + 1)
                dve.tensor_reduce(nmax[:, row, 0:1], prob[:, base + 2 * nk:base + 2 * nk + NCMP], X, ALU.max,
                                  negate=True).then_inc(nm_ok, 1)

            def weighted(u, base, nk, gate):
                row = 1 if base else 0
                dve.wait_ge(ex_ok, u + 1)
                V.add(dve.reciprocal(wgt[:, row, 0:3], sums[:, row, 0:3]))
                V.sync()
                V.add(TT(wgt[:, row, 0:3], wgt[:, row, 0:3], gate, ALU.mult))
                V.sync()
                for b in range(3):
                    w = prob[:, base + b * nk:base + (b + 1) * nk] if b < 2 else \
                        prob[:, base + 2 * nk:base + 2 * nk + NCMP]
                    ins = TS(w, w, wgt[:, row, BR[b]:BR[b] + 1], None, ALU.mult)
                    if b < 2:
                        V.add(ins)
                    else:
                        ins.then_inc(pn_ok, 1)

            for g in range(GROUPS):
                def turn(hh):
                    u0, h = hh * 2 + 8 * g, hh + 4 * g
                    for qt in range(2):
                        nk = (qt + 1) * P
                        off = P if qt == 0 else 0
                        scored(u0 + qt, qt * PW, nk,
                               ps[:, 2 + qt, 0:2 * nk].rearrange("p (b k) -> p b k", b=2),
                               bias_p[:, ds(h, 1), off:off + nk].to_broadcast([P, 2, nk]),
                               ps[:, 4 + qt, 0:NCMP],
                               bias_pc[:, qt, ds(h, 1), :].rearrange("p o k -> p (o k)"))
                    for qt in range(2):
                        weighted(u0 + qt, qt * PW, (qt + 1) * P, gate_p[:, qt, ds(h * 3, 3)])
                    for qt in range(2):
                        dve.wait_ge(oh_ok, u0 + (qt + 1))
                        sl = (slice(None), ds(h, 1), slice(qt * P, qt * P + P))
                        TT(oL[sl], ps[:, qt:qt + 1, 0:P], oH[sl].bitcast(F32), ALU.subtract).then_inc(ol_ok, 1)

                turns(dve, HPG, turn, V)
            for k in range(4):
                g, bh = k // 2, k % 2
                u = 16 + k
                scored(u, 0, T, ps[:, 2:4, 0:T], bias_s[:, k:k + 1, :].to_broadcast([P, 2, T]), ps[:, 4, 0:NCMP],
                       bias_sc[:, k, :])
                weighted(u, 0, T, gate_s[:, k, :])
                dve.wait_ge(oh_ok, u + 1)
                for h4 in range(4):
                    sl = (slice(None), 4 * g + h4, slice(SEQ + 32 * bh, SEQ + 32 * bh + 32))
                    ins = TT(oL[sl].rearrange("p (j s) -> p j s", j=4),
                             ps[:, 0, 0:P].rearrange("p (j h s) -> p j h s", j=4, h=4)[:, :, h4, :],
                             oH[sl].bitcast(F32).rearrange("p (j s) -> p j s", j=4), ALU.subtract)
                    if h4 < 3:
                        V.add(ins)
                ins.then_inc(ol_ok, 1)

            lb, oml = lbx[:, 0, :], lbx[:, 1, :]

            def tail1(h):
                dve.wait_ge(t_ok, h + 1)
                for i in range(3):
                    m = P if i < 2 else SMP
                    ins = TT(vmask[0:m, i], v_tok[0:m, i:i + 1, :].to_broadcast([m, 8, P]),
                             c_("chunk_p" if i < 2 else "chunk_s")[0:m, :].unsqueeze(2).to_broadcast([m, 8, P]),
                             ALU.mult)
                    V.add(ins)
                mask = c_("causal_p").bitcast(U32)
                for i in range(2):
                    V.add(dve.copy_predicated(att[:, i * P:i * P + P], mask, ps[:, 4, i * P:i * P + P]))
                dve.copy_predicated(att[0:SMP, SEQ:T], c_("causal_s")[0:SMP, :].bitcast(U32),
                                    ps[0:SMP, 4, SEQ:T]).then_inc(m_ok, 1)

            def tail2(h, par, turn):
                if later(turn * 32):
                    dve.wait_ge(st_out[par], turn * 32)
                for c in range(16):
                    if c in (0, 8):
                        dve.wait_ge(u_ps, h * 3 + (1 if c == 0 else 2))
                    U = ps[:, (5, 6, 7, 2)[c // 4], (c % 4) * P:(c % 4) * P + P]
                    out = st[:, c + 1, :] if c < 15 else sfin[:, par, :]
                    if c == 0:
                        V.add(dve.tensor_copy(out, U))
                    else:
                        V.sync()
                        V.add(STT(out, st[:, c, :], cum[:, par, HC * c + HC - 1:HC * c + HC], U, ALU.mult, ALU.add))
                dve.wait_ge(u_ps, h * 3 + 3)
                dve.wait_ge(s0_in[par], turn * 16 + 16)
                for b in range(DB):
                    last = SEQ + DS * b + DS - 1
                    ins = STT(sn[:, par, b, :], s0[:, par, b, :], cum[:, par, last:last + 1],
                              ps[:, 3 + b // 4, (b % 4) * P:(b % 4) * P + P], ALU.mult, ALU.add)
                    if b < DB - 1:
                        V.add(ins)
                ins.then_inc(s_ok, 1)

            def tail3(h, par):
                dve.wait_ge(hm_ps, h + 1)
                V.add(TS(orn[:], ps[:, 6, 0:T], EPS, None, ALU.add))
                V.sync()
                dve.reciprocal(orn[:], orn[:]).then_inc(hv_ok, 1)
                dve.wait_ge(hr_ok, h + 1)
                V.add(STT(osb[:], osb[:], hgn, orn[:], ALU.mult, ALU.mult))
                V.sync()
                TT(osb[:], osb[:], ogs[:, par, :], ALU.mult).then_inc(hn_ok, 1)
                dve.wait_ge(hoh, h + 1)
                TT(oL[:, ds(h + 8, 1), :], osb[:].rearrange("p (o t) -> p o t", o=1),
                   oH[:, ds(h + 8, 1), :].bitcast(F32), ALU.subtract).then_inc(hol, 1)

            def window(h, par, i=None, k=0):
                n = N_HG + 4 * k
                nn = n if i is None else i * 8 + n
                turn = (k - 1) // 2 if i is None else i + (k - 1) // 2
                if k:
                    tail1(h - 1)
                split_after(n, i, 8)
                if k:
                    tail2(h - 1, 1 - par, turn)
                dve.wait_ge(free[0], h * 2 + (R_HG // 2 + 1))
                V.add(TS(fsig[:], fsig[:], oml[:, ds(h, 1)], lb[:, ds(h, 1)], ALU.mult, ALU.add))
                V.add(TS(nsig[:], nsig[:], oml[:, ds(h, 1)], None, ALU.mult))
                V.sync()
                V.add(TT(fmul[:], fsig[:], c_("seg"), ALU.mult))
                V.sync()
                V.add(TT(fset[:], fsig[:], fmul[:], ALU.subtract))
                V.sync()
                V.add(dve.tensor_tensor_scan(cum[:, par, :], fmul[:], fset[:], 0.0, ALU.mult, ALU.add))
                V.sync()
                V.add(dve.reciprocal(fmul[:], cum[:, par, :]))
                V.sync()
                V.add(TT(kinv[:, par, :], nsig[:], fmul[:], ALU.mult))
                V.sync()
                V.add(TT(kend[:, par, 0:SEQ].rearrange("p (c s) -> p c s", s=HC),
                         kinv[:, par, 0:SEQ].rearrange("p (c s) -> p c s", s=HC),
                         cum[:, par, 0:SEQ].rearrange("p (c s) -> p c s", s=HC)[:, :, HC - 1:HC].to_broadcast([P, 16, HC]),
                         ALU.mult))
                TT(kend[:, par, SEQ:T].rearrange("p (c s) -> p c s", s=DS),
                   kinv[:, par, SEQ:T].rearrange("p (c s) -> p c s", s=DS),
                   cum[:, par, SEQ:T].rearrange("p (c s) -> p c s", s=DS)[:, :, DS - 1:DS].to_broadcast([P, DB, DS]),
                   ALU.mult).then_inc(f_done, 1)
                split_after(n + 1, i, 8)
                split_after(n + 2, i, 8)
                TT(qdec[:, par, :], ps[:, 0, 0:T], cum[:, par, :], ALU.mult).then_inc(free[0], 1)
                if k:
                    tail3(h - 1, 1 - par)
                split_after(n + 3, i, 8)
                dve.wait_ge(o_sig, h + 1)
                TT(ogs[:, par, :], ps[:, 1, 0:T], osig[:], ALU.mult).then_inc(free[1], 1)

            dve.wait_ge(kv_out, 16 * 13)
            V.add(dve.memset(att[:], 0.0))
            V.sync()
            window(0, 0)
            window(1, 1, None, 1)
            window(2, 0, None, 2)
            with V.loop(2, 2 * (8 + 5 + 23 + 2)) as i:
                window(i * 2 + 3, 1, i, 3)
                window(i * 2 + 4, 0, i, 4)
            window(7, 1, None, 7)
            tail1(7)
            tail2(7, 1, 3)
            tail3(7, 1)

            for par in range(2):
                dve.wait_ge(st_out[par], 16 * HEADS)
            def turn(j):
                for v in range(2):
                    m, n = j * 2 + v, N_MRG + 3 * v
                    for u in range(3):
                        c = n + u + 2
                        split(j * 6 + c, c % 2)
                    dve.wait_ge(mg_a, m * 2 + 2)
                    dve.wait_ge(used, j * 6 + (n + 3))
                    V.add(TT(mix[:, v, :], sga[:, v, :], ps[:, 4 * v + 2, 0:T], ALU.mult))
                    TT(mix2[:, v, :], sgb[:, v, :], ps[:, 4 * v + 3, 0:T], ALU.mult).then_inc(mg_rd[v], 1)
                    V.sync()
                    dve.wait_ge(mg_rd[v], j + 1)
                    TT(mix[:, v, :], mix[:, v, :], mix2[:, v, :], ALU.add).then_inc(mg_mix, 1)
                    dve.wait_ge(mg_hi, m + 1)
                    TT(mL[:, ds(m, 1), :], mix[:, v:v + 1, :], mH[:, ds(m, 1), :].bitcast(F32), ALU.subtract
                       ).then_inc(mg_lo, 1)

            turns(dve, KT//2, turn, V)
            V.add(dve.memset(sqs[:], 0.0))
            V.sync()
            def turn(j):
                for u in range(2):
                    m = j * 2 + u
                    split_after(N_OUT + u, j, 2)
                    dve.wait_ge(y_sq, m + 1)
                    if later(m):
                        dve.wait_ge(y_add, m)
                    TT(sqs[:], sqs[:], sq[:, u, :], ALU.add).then_inc(y_add, 1)

            turns(dve, KT//2, turn)

            def rstd(k):
                dve.wait_ge(mean_ps, k)
                V.add(TS(rsb[:], ps[:, 2, 0:T], EPS, None, ALU.add))
                V.add(dve.memset(sqs[:], 0.0))
                V.sync()
                dve.reciprocal(rsb[:], rsb[:]).then_inc(mean_v, 1)
                dve.wait_ge(rstd_ok, k)

            def normed(out, in_, n, k):
                V.add(STT(out[:, k, :], in_[:, k, :], ln[:, n, k:k + 1], rsb[:], ALU.mult, ALU.mult))
                V.sync()

            rstd(1)
            dve.wait_ge(x1_in, 16)
            dve.wait_ge(free[0], R_FFN // 2)
            dve.wait_ge(free[1], R_FFN // 2)
            for k in range(KT + 1):
                if k < KT:
                    normed(y1, y1, 1, k)
                    TT(x1[:, k, :], x1[:, k, :], y1[:, k, :], ALU.add).then_inc(x_new, 1)
                if k:
                    dve.wait_ge(x_sq, k)
                    if k > 1:
                        dve.wait_ge(x_add, k - 1)
                    TT(sqs[:], sqs[:], sq[:, (k - 1) % 2, :], ALU.add).then_inc(x_add, 1)
            rstd(2)
            for k in range(KT + 1):
                if k < KT:
                    STT(y1[:, k, :], x1[:, k, :], ln[:, 2, k:k + 1], rsb[:], ALU.mult, ALU.mult).then_inc(h_new, 1)
                if k:
                    dve.wait_ge(h2h, k)
                    TT(hL[:, k - 1, :], y1[:, k - 1, :], hH[:, k - 1, :].bitcast(F32), ALU.subtract).then_inc(h2l, 1)

            dve.wait_ge(h2l, KT)
            V.add(dve.memset(ue[:, :, :, 0:2], 0.0))
            V.sync()
            n0, r0, i0 = N_FFN, R_FFN, 0
            for part, cnt in enumerate(PARTS):
                def turn(j):
                    for par in range(2):
                        i = j * 2 + (i0 + par)
                        for s in range(2):
                            dve.tensor_copy(ue[:, par, s, 2 + SEQ:UW].rearrange("p (b c) -> p b c", b=DB)[:, :, 0:2],
                                            hist[:, ds(i + s * FT, 1), :].rearrange("p o (b c) -> p (o b) c", b=DB)
                                            ).then_inc(u_hist, 1)
                        for s in range(2):
                            col = i + s * FT
                            split_after(n0 + 2 * par + s, j, 4)
                            dve.wait_ge(u_ev, i * 2 + (s + 1))
                            V.add(STT(cc[:, s, :], ue[:, par, s, 1:UW - 1], conv[:, 1, ds(col, 1)], cc[:, s, :],
                                      ALU.mult, ALU.add))
                            V.sync()
                            STT(cc[:, s, :], ue[:, par, s, 2:UW], conv[:, 2, ds(col, 1)], cc[:, s, :],
                                ALU.mult, ALU.add).then_inc(c_ok, 1)
                            V.add(dve.tensor_copy(newc[:, ds(col, 1), :].rearrange("p o (b c) -> p (o b) c", b=NSEQ),
                                                  ue[:, par, s, UW - 90:UW].rearrange("p (b c) -> p b c", b=NSEQ)[:, :, 8:]))
                        dve.wait_ge(g_ok, i + 1)
                        if later(i):
                            dve.wait_ge(a_hi, i)
                        V.add(TT(gg[:, 0:SEQ], cc[:, 0, 0:SEQ], cc[:, 1, 0:SEQ], ALU.mult))
                        TT(gg[:, SEQ:T].rearrange("p (b c) -> p b c", b=DB),
                           cc[:, 0, SEQ:UW - 2].rearrange("p (b c) -> p b c", b=DB)[:, :, 2:],
                           cc[:, 1, SEQ:UW - 2].rearrange("p (b c) -> p b c", b=DB)[:, :, 2:], ALU.mult
                           ).then_inc(m_new, 1)
                        dve.wait_ge(a_hi, i + 1)
                        TT(aL[:, ds(j * 2 + par, 1), :], gg[:].rearrange("p (o t) -> p o t", o=1),
                           aH[:, ds(j * 2 + par, 1), :].bitcast(F32), ALU.subtract).then_inc(a_lo, 1)

                turns(dve, cnt//2, turn, V)
                n0 += 2 * cnt
                r0 += 2 * cnt
                i0 += cnt

                def down(m, u, j, last):
                    dve.wait_ge(used, m + (n0 + 1))
                    tile = acc[:, ds(m, 1), :]
                    if part == 0:
                        dve.tensor_copy(tile, ps[:, u:u + 1, 0:T]).then_inc(free[u], 1)
                    else:
                        TT(tile, tile, ps[:, u:u + 1, 0:T], ALU.add).then_inc(free[u], 1)
                    if part == 2:
                        dve.wait_ge(d_sq, m + 1)
                        if later(m):
                            dve.wait_ge(d_add, m)
                        TT(sqs[:], sqs[:], sq[:, u, :], ALU.add).then_inc(d_add, 1)

                def turn(j):
                    for u in range(2):
                        split_after(n0 + u, j, 2)
                        down(j * 2 + u, u, j, False)

                turns(dve, KT//2-(part==2), turn)
                if part == 2:
                    for u in range(2):
                        down(KT - 2 + u, u, KT // 2 - 1, True)
                n0 += KT
                r0 += KT
            rstd(3)
            for k in range(KT):
                normed(acc, acc, 3, k)
                TT(acc[:, k, :], acc[:, k, :], x1[:, k, :], ALU.add).then_inc(y_fin, 1)

        @block.tensor
        def _(pe):
            def product(out, lhsT, rhs, start=True, stop=True):
                return pe.matmul(out, lhsT, rhs, start=start, stop=stop, skip_group_check=True)

            def gemm(n, slot, out, xH, xL, tiles, wait=True, done=True):
                if wait:
                    pe.wait_ge(lo_ready, n + 1)
                last = len(tiles) - 1
                for q, (w, k) in enumerate(tiles):
                    for p_, (ww, xx) in enumerate(((whi, xH), (whi, xL), (wlo, xH))):
                        ins = pe.matmul(out, ww[:, slot, w, :], xx[:, k, :],
                                        start=(q == 0 and p_ == 0), stop=(q == last and p_ == 2),
                                        skip_group_check=True)
                if done:
                    ins.then_inc(used, 1)
                return ins

            all16 = [(k, k) for k in range(16)]

            pe.wait_ge(cst_in, 16)
            pe.wait_ge(rows_in, 16 * 8)
            pe.transpose(ps[:, 1, 0:81], rows[0:81, :], ident[0:81, 0:81])
            for n in range(4):
                ins = pe.transpose(ps[:, 1, 81 + 88 * n:81 + 88 * n + 88], crow[:, n, :], ident[0:88, 0:88])
            ins.then_inc(par_ps, 1)
            pe.wait_ge(x_in, 48)
            for k in range(KT):
                if k >= 6:
                    pe.wait_ge(xt_ok, k - 5)
                for i in range(3):
                    m = P if i < 2 else SMP
                    ins = pe.transpose(ps[:, 2 + k % 6, i * P:i * P + m], xtok[0:m, i, k * P:k * P + P],
                                       ident[0:m, 0:m])
                ins.then_inc(xt_ps, 1)
                if k == 5:
                    pe.wait_ge(rs_ok, 1)
                    for i in range(3):
                        m = P if i < 2 else SMP
                        ins = product(ps[:, 0, i * P:i * P + m], stat[0:m, 3 + i:4 + i].to_broadcast([m, P]),
                                      ident[0:m, 0:m])
                    ins.then_inc(rsb_ps, 1)
            pe.wait_ge(hl_ok, KT)
            pe.wait_ge(par_ok, 1)
            pe.wait_ge(rsb_ok, 1)
            def turn(j):
                for u in range(2):
                    if later(j):
                        pe.wait_ge(free[u], j)
                    gemm(j * 2 + u, u, ps[:, u, 0:T], hH, hL, all16)

            turns(pe, N_A//2, turn)
            pe.wait_ge(lo_ready, N_GATE + 1)
            for i, t0 in enumerate((0, P, T - P)):
                for k in range(KT):
                    for p_, (xx, ww) in enumerate(((hH, whi), (hL, whi), (hH, wlo))):
                        ins = product(ps[:, 2, i * 24:i * 24 + 24], xx[:, k, t0:t0 + P], ww[:, N_GATE % 2, k, 0:24],
                                      start=(k == 0 and p_ == 0), stop=(k == 15 and p_ == 2))
            ins.then_inc(used, 1)
            pe.wait_ge(w2_in, 32)
            for c in range(2):
                ins = pe.transpose(ps[:, 4, c * BLK:c * BLK + BLK], pe_row[:, c, :], ident[0:BLK, 0:BLK])
            ins.then_inc(pe_ps, 1)
            pe.wait_ge(free[0], N_A // 2)
            pe.wait_ge(free[1], N_A // 2)
            for f in range(12):
                if f >= 2:
                    pe.wait_ge(tok_ok, f - 1)
                for i in range(3):
                    m = P if i < 2 else SMP
                    ins = pe.transpose(ps[0:m, f % 2, i * P:i * P + P], kvq[:, f, i * P:i * P + m], ident)
                ins.then_inc(tok_ps, 1)
            pe.wait_ge(pe_ok, 1)
            def turn(j):
                for u in range(4):
                    pe.wait_ge(page_in[u], j * 16 + 16)
                    pe.wait_ge(page_ok, j * 4 + 1)
                    for c in range(4):
                        ins = pe.transpose(ps[:, 4 + u, c * P:c * P + P], page[:, u, c * P:c * P + P], ident)
                    ins.then_inc(page_ps, 1)

            turns(pe, DB//2, turn)
            pe.wait_ge(gate_ok, 1)
            pe.wait_ge(cat_in, 16)
            for bh in range(2):
                ins = product(ps[:, 3, bh * 24:bh * 24 + 24], pick[:, bh, :], gates[:, 2, :])
            ins.then_inc(gsel_ps, 1)
            pe.wait_ge(tok_ok, 12)
            pe.wait_ge(page_ok, 17)
            blocks = kcT[:].rearrange("p (c g) s (b l) -> p c l (g s b)", c=2, l=BLK)
            for c in range(2):
                for q in range(4):
                    n = N_CMP + 4 * c + q
                    pe.wait_ge(lo_ready, n + 1)
                    for l in range(16):
                        ins = product(ps[:, c, 0:NCMP], raw[:, n % 2, l, :], blocks[:, c, 16 * q + l, :],
                                      start=(q == 0 and l == 0), stop=(q == 3 and l == 15))
                    ins.then_inc(used, 1)
            pe.wait_ge(hid_ok, 2)
            pe.wait_ge(gsel_ok, 1)
            product(ps[:, 2, 0:NCMP], w2[:, 0, :], hid[:, 0, :])
            product(ps[0:NCMP, 3, 0:P], hid[:, 1, :], w2[:, 1, :]).then_inc(cc_ps, 1)
            pe.wait_ge(cc_ok, 2)

            PW = 512 + NCMP
            for g in range(GROUPS):
                def turn(hh):
                    u0 = hh * 2 + 8 * g
                    pe.wait_ge(q_ok, hh + (4 * g + 1))
                    if later(u0):
                        pe.wait_ge(sc_rd, u0)
                    for qt in range(2):
                        nk = (qt + 1) * P
                        q = qst[:, qt * P:qt * P + P]
                        product(ps[:, 2 + qt, 0:nk], q, kvq[:, 4 + g, 0:nk])
                        product(ps[:, 2 + qt, nk:2 * nk], q, kvq[:, 8 + g, 0:nk])
                        product(ps[:, 4 + qt, 0:NCMP], q, ckT[:]).then_inc(sc_ps, 1)
                    for qt in range(2):
                        base, nb = qt * PW, 2 * (qt + 1)
                        pe.wait_ge(pn_ok, u0 + (qt + 1))
                        if later(u0 + qt):
                            pe.wait_ge(pt_ok, u0 + qt)
                        for b in range(nb):
                            pe.transpose(ps[:, 6, b * P:b * P + P], prob[:, base + b * P:base + b * P + P], ident)
                        pe.transpose(ps[0:NCMP, 7, 0:P], prob[:, base + nb * P:base + nb * P + NCMP], ident
                                     ).then_inc(pt_ps, 1)
                        pe.wait_ge(pt_ok, u0 + (qt + 1))
                        if later(u0):
                            pe.wait_ge(ol_ok, u0)
                        out = ps[:, qt, 0:P]
                        for br, col in enumerate((6 + g, 10 + g)):
                            for kt in range(qt + 1):
                                product(out, kvtok[:, kt, col * P:col * P + P], pT[qt][:, br * (qt + 1) + kt, :],
                                        start=(br == 0 and kt == 0), stop=False)
                        product(out, cv[0:NCMP, :], pTc[0:NCMP, qt, :], start=False).then_inc(ov_ps, 1)

                turns(pe, HPG, turn)
            pe.wait_ge(q_ok, HEADS + 1)
            for k in range(4):
                g, u = k // 2, 16 + k
                if later(u):
                    pe.wait_ge(sc_rd, u)
                if later(u):
                    pe.wait_ge(pt_ok, u)
                for br, (kv, arrived) in enumerate(((kv_sel, sel_in), (kv_win, win_in))):
                    pe.wait_ge(arrived, 128 * (k + 1))
                    if br:
                        pe.wait_ge(kt_ok, 2 * k + 1)
                    for j in range(4):
                        for t in range(2):
                            b = 2 * j + t
                            ins = pe.transpose(ps[:, 5 + b // 4, (b % 4) * P:(b % 4) * P + P], kv[:, j, 2 * t, :], ident)
                    ins.then_inc(kt_ps, 1)
                    pe.wait_ge(kt_ok, 2 * k + br + 1)
                    for j in range(4):
                        product(ps[32 * j:32 * j + 32, 2 + br, 0:PAST], qs[:, k, 32 * j:32 * j + 32],
                                KTs[:, 2 * j:2 * j + 2, :].rearrange("p a d -> p (a d)"))
                    product(ps[:, 2 + br, PAST:T], qs[:, k, :], kvq[:, (4, 8)[br] + g, SEQ:T]).then_inc(ks_ps, 1)
                product(ps[:, 4, 0:NCMP], qs[:, k, :], ckT[:]).then_inc(sc_ps, 1)
                pe.wait_ge(pn_ok, u + 1)
                for br in range(2):
                    for t in range(3):
                        m = P if t < 2 else SMP
                        pe.transpose(ps[0:m, 5 + br, t * P:t * P + P], prob[:, br * T + t * P:br * T + t * P + m], ident)
                pe.transpose(ps[0:NCMP, 7, 0:P], prob[:, 2 * T:2 * T + NCMP], ident).then_inc(pt_ps, 1)
                pe.wait_ge(pt_ok, u + 1)
                if later(u):
                    pe.wait_ge(ol_ok, u)
                for br, col in enumerate((6 + g, 10 + g)):
                    product(ps[:, 0, 0:P], kvtok[0:SMP, 2, col * P:col * P + P], pTs[0:SMP, 3 * br + 2, :],
                            start=(br == 0), stop=False)
                product(ps[:, 0, 0:P], cv[0:NCMP, :], pTs[0:NCMP, 6, :], start=False, stop=False)
                for br, kv in enumerate((kv_sel, kv_win)):
                    for j in range(4):
                        for t in range(2):
                            ins = product(ps[:, 0, 32 * j:32 * j + 32], kv[:, j, 2 * t + 1, :],
                                          pTs[:, 3 * br + t, 32 * j:32 * j + 32], start=False,
                                          stop=(br == 1 and t == 1))
                ins.then_inc(ov_ps, 1)

            def tail1(h, par):
                pe.wait_ge(f_done, h + 1)
                pe.wait_ge(free[1], h * 2 + (R_HG // 2 + 1))
                pe.wait_ge(free[0], h * 2 + (R_HG // 2 + 2))
                if later(h):
                    pe.wait_ge(s_ok, h)
                for bank, src in ((2, kend), (3, vT)):
                    for i in range(3):
                        m = P if i < 2 else SMP
                        pe.transpose(ps[0:m, bank, i * P:i * P + P], src[:, par, i * P:i * P + m], ident)
                for i in range(3):
                    m = P if i < 2 else SMP
                    sl = slice(i * P, i * P + m)
                    ins = product(ps[0:m, 4, sl], kinv[:, par, sl], qdec[:, par, sl])
                ins.then_inc(t_ps, 1)

            def tail2(h):
                pe.wait_ge(m_ok, h + 1)
                if later(h):
                    pe.wait_ge(ho_sb, h)
                if later(h):
                    pe.wait_ge(hv_ok, h)
                for i, banks in enumerate(((5, 6), (7, 2), (3, 4))):
                    m = P if i < 2 else SMP
                    for q, bank in enumerate(banks):
                        ins = product(ps[:, bank, :], kend_tok[0:m, i, :],
                                      vmask[0:m, i, 4 * q:4 * q + 4, :].rearrange("p c d -> p (c d)"))
                    ins.then_inc(u_ps, 1)

            def tail3(h, par):
                pe.wait_ge(s_ok, h + 1)
                for i in range(3):
                    m = P if i < 2 else SMP
                    sl = slice(i * P, i * P + m)
                    product(ps[:, 5, sl], v_tok[0:m, i, :], att[0:m, sl], start=(i == 0), stop=False)
                for c in range(1, 16):
                    sl = slice(HC * c, HC * c + HC)
                    product(ps[:, 5, sl], st[:, c, :], qdec[:, par, sl], start=False, stop=False)
                for b in range(DB):
                    sl = slice(SEQ + DS * b, SEQ + DS * b + DS)
                    ins = product(ps[:, 5, sl], s0[:, par, b, :], qdec[:, par, sl], start=False, stop=(b == DB - 1))
                ins.then_inc(ho_ps, 1)

            def tail4(h):
                pe.wait_ge(ho_sb, h + 1)
                product(ps[:, 6, 0:T], c_("mean_h"), osq[:]).then_inc(hm_ps, 1)

            def window(h, par, i=None, k=0):
                n = N_HG + 4 * k
                nn = n if i is None else i * 8 + n
                if k:
                    tail1(h - 1, 1 - par)
                for u in range(4):
                    pe.wait_ge(free[u % 2], h * 2 + (R_HG // 2 + u // 2))
                    gemm(nn + u, (n + u) % 2, ps[:, u % 2, 0:T], hH, hL, all16)
                    if k and u == 0:
                        tail2(h - 1)
                    if k and u == 1:
                        tail3(h - 1, 1 - par)
                    if k and u == 2:
                        tail4(h - 1)

            pe.wait_ge(ol_ok, 20)
            window(0, 0)
            window(1, 1, None, 1)
            window(2, 0, None, 2)
            with pe.Fori(0, 2) as i:
                window(i * 2 + 3, 1, i, 3)
                window(i * 2 + 4, 0, i, 4)
            window(7, 1, None, 7)
            tail1(7, 1)
            tail2(7)
            tail3(7, 1)
            tail4(7)

            pe.wait_ge(hol, HEADS)
            pe.wait_ge(hv_ok, HEADS)
            pe.wait_ge(s_ok, HEADS)
            def turn(j):
                for v in range(2):
                    n = N_MRG + 3 * v
                    if later(j):
                        pe.wait_ge(mg_rd[v], j)
                    gemm(j * 6 + n, n % 2, ps[:, 4 * v, 0:T], hH, hL, all16)
                    gemm(j * 6 + (n + 1), (n + 1) % 2, ps[:, 4 * v + 1, 0:T], hH, hL, all16)
                    gemm(j * 6 + (n + 2), (n + 2) % 2, ps[:, 4 * v + 2, 0:T], oH, oL,
                         [(k, k) for k in range(8)], done=False)
                    gemm(j * 6 + (n + 2), (n + 2) % 2, ps[:, 4 * v + 3, 0:T], oH, oL,
                         [(k, k) for k in range(8, 16)], wait=False)

            turns(pe, KT//2, turn)
            pe.wait_ge(mg_lo, KT)
            def turn(j):
                for u in range(2):
                    pe.wait_ge(free[u], j + R_OUT // 2)
                    gemm(j * 2 + (N_OUT + u), (N_OUT + u) % 2, ps[:, u, 0:T], mH, mL, all16)

            turns(pe, KT//2, turn)
            pe.wait_ge(hrow_in, 16)
            for i in range(4):
                for q in range(4):
                    ins = pe.transpose(ps[:, 3 + i, q * 2 * FT:(q + 1) * 2 * FT], hrow[:, 4 * i + q, :],
                                       ident[0:2 * FT, 0:2 * FT])
                ins.then_inc(hist_ps, 1)
            for done, count in ((y_add, KT), (x_add, KT)):
                pe.wait_ge(done, count)
                product(ps[:, 2, 0:T], c_("mean_d"), sqs[:]).then_inc(mean_ps, 1)
            pe.wait_ge(h2l, KT)
            pe.wait_ge(hist_ok, 4)
            n0, r0, i0 = N_FFN, R_FFN, 0
            for part, cnt in enumerate(PARTS):
                def turn(i):
                    for s in range(2):
                        pe.wait_ge(free[s], i + r0 // 2)
                        gemm(i * 2 + (n0 + s), (n0 + s) % 2, ps[:, s, 0:T], hH, hL, all16)

                turns(pe, cnt, turn)
                n0 += 2 * cnt
                r0 += 2 * cnt
                i0 += cnt
                pe.wait_ge(a_lo, i0)
                if part == 2:
                    for i in range(5):
                        for q in range(4 * i, min(4 * i + 4, 2 * NSEQ)):
                            ins = pe.transpose(ps[0:2 * FT, 3 + i, (q - 4 * i) * P:(q - 4 * i + 1) * P],
                                               newc[:, :, q], ident)
                        ins.then_inc(nc_ps, 1)
                def turn(j):
                    for u in range(2):
                        pe.wait_ge(free[u], j + r0 // 2)
                        gemm(j * 2 + (n0 + u), (n0 + u) % 2, ps[:, u, 0:T], aH, aL, [(k, k) for k in range(cnt)])

                turns(pe, KT//2, turn)
                n0 += KT
                r0 += KT
            pe.wait_ge(d_add, KT)
            product(ps[:, 2, 0:T], c_("mean_d"), sqs[:]).then_inc(mean_ps, 1)
            pe.wait_ge(nc_ok, 5)
            for k in range(KT):
                pe.wait_ge(y_fin, k + 1)
                if k >= 4:
                    pe.wait_ge(yt_ok, k - 3)
                for i in range(3):
                    m = P if i < 2 else SMP
                    ins = pe.transpose(ps[0:m, 3 + k % 4, i * P:i * P + P], acc[:, k, i * P:i * P + m], ident)
                ins.then_inc(yt_ps, 1)


def constants():
    import numpy as np

    def put(out, spec, name, value):
        v = np.asarray(value, np.float32)
        v = v.reshape(v.shape[0], -1)
        out[:v.shape[0], spec[name]] = v

    p = np.arange(P)
    t = np.arange(T)
    c = np.zeros((P, CP_N), np.float32)
    put(c, CP, "ident", np.eye(P))
    put(c, CP, "mean_d", np.full((P, P), 1.0 / D))
    put(c, CP, "mean_h", np.full((P, P), 1.0 / P))
    starts = np.where(t < SEQ, t % HC == 0, (t - SEQ) % DS == 0)
    put(c, CP, "seg", np.broadcast_to(1.0 - starts, (P, T)))
    put(c, CP, "causal_p", (p[:, None] // HC == p // HC) & (p[:, None] <= p))
    s = np.arange(SMP)
    put(c, CP, "causal_s", (s[:, None] // DS == s // DS) & (s[:, None] <= s))
    put(c, CP, "chunk_p", p[:, None] // HC == np.arange(8))
    put(c, CP, "chunk_s", s[:, None] // DS == np.arange(8))

    a = np.zeros((P, CA_N), np.float32)
    slope = 2.0 ** -(np.arange(HEADS) + 1.0)

    def bias(slopes, dist, ok):
        return np.where(ok & (dist >= 0), -slopes * dist, NEG)

    dist = p[:, None] - (np.arange(2 * P) - P)
    put(a, CA, "bias_p", bias(slope[None, :, None], dist[:, None, :], True))
    g, q, b = np.meshgrid(np.arange(GROUPS), np.arange(NSEQ), np.arange(NBLK), indexing="ij")
    g, q, end = g.ravel(), q.ravel(), (b.ravel() + 1) * BLK - 1
    pos = np.arange(2)[None, :] * P + p[:, None]
    put(a, CA, "bias_pc", bias(slope[None, None, :, None], (pos[:, :, None] - end)[:, :, None, :],
                               (q == 0) & (g == (np.arange(HEADS) // HPG)[:, None])))
    put(a, CA, "valid", np.stack([pos >= BLK - 1, pos >= 0, pos >= 0], -1))
    j, hh, ss = p // 32, p // DS % HPG, p % DS
    bs, bsc = [], []
    for k in range(4):
        gk, seq = k // 2, 4 * (k % 2) + j
        sl = slope[4 * gk + hh][:, None]
        bs.append(np.concatenate([bias(sl, PAST + ss[:, None] - np.arange(PAST), True),
                                  bias(sl, ss[:, None] - s % DS, s // DS == seq[:, None])], 1))
        bsc.append(bias(sl, PAST + ss[:, None] - end, (g == gk) & (q == 1 + seq[:, None])))
    put(a, CA, "bias_s", np.stack(bs, 1))
    put(a, CA, "bias_sc", np.stack(bsc, 1))
    rows = p[:, None] - (P - SMP)
    put(a, CA, "pick", np.stack([rows == (4 * bh + j) * DS + ss for bh in range(2)], 1))
    put(a, CA, "head", np.broadcast_to(hh[:, None, None] == np.arange(4)[:, None], (P, 4, 3)))
    return c, a


_OUTS = [(1, SEQ, D), (DB, DS, D)] + [s for _ in range(2) for s in
                                      ((1, 1, SEQ, 2, GROUPS, P), (1, DB, DS, 2, GROUPS, P))] + [
    (1, 1, SEQ, 2, GROUPS, P), (1, DB, PAST, 2, GROUPS, P),
    (1, 1, HEADS, P, P), (1, DB, HEADS, P, P), (1, 1, 2, 2 * DFF), (1, DB, 2, 2 * DFF)]


def kernel(**inputs):
    import numpy as np
    import concourse.bacc as bacc
    from concourse.bass_utils import run_bass_kernel_spmd as run

    nc = bacc.Bacc("TRN2", target_bir_lowering=False, num_devices=1)
    const, att_const = constants()
    arrays, aps = {}, {}
    for name, v in {**inputs, "const": const, "att_const": att_const}.items():
        v = np.ascontiguousarray(v)
        arrays[f"in_{name}"] = v
        aps[name] = nc.dram_tensor(f"in_{name}", v.shape, mybir.dt.from_np(v.dtype), kind="ExternalInput").ap()
    outs = [nc.dram_tensor(f"out_{i}", shape, F32, kind="ExternalOutput").ap() for i, shape in enumerate(_OUTS)]
    xt = nc.dram_tensor("x_feature_major", (P, KT * T), F32, kind="Internal").ap()
    layer(nc, aps, outs, xt)
    r = run(nc, [arrays], core_ids=[0])
    return tuple(r.results[0][f"out_{i}"] for i in range(len(_OUTS)))
```

```python
from contextlib import ExitStack, contextmanager

import concourse.bass as bass
from concourse import mybir

F32 = mybir.dt.float32
F32R = mybir.dt.float32r
I32 = mybir.dt.int32
U32 = mybir.dt.uint32
ALU = mybir.AluOpType
ACT = mybir.ActivationFunctionType
X = mybir.AxisListType.X
ds = bass.ds

P = 128
D = 2048
KT = D // P
SEQ, DB, DS = 256, 8, 8
SMP = DB * DS
T = SEQ + SMP
PAST, PAGE = 256, 128
N_PHYS = 20
HEADS, GROUPS, HPG = 8, 2, 4
BLK = 64
NBLK = PAST // BLK
NSEQ = 1 + DB
NCMP = GROUPS * NSEQ * NBLK
DFF = 5632
FT = DFF // P
UW = 2 + SEQ + DB * (DS + 2)
EPS = 1e-6
NEG = -1e30
SCALE = P ** -0.5
HC = 16
COL_KV, COL_GATE = 1024, 2560
COL_HQ, COL_HF, COL_HI, COL_HO, COL_MRG = 2584, 3608, 4632, 5656, 6680

N_A = 20
N_GATE = N_A
N_CMP = N_GATE + 1
N_MG = N_CMP + 8
M_LATE = KT - 2
N_HG = N_MG + 2 * M_LATE
N_MG2 = N_HG + 4 * HEADS
N_AB = N_MG2 + 2 * (KT - M_LATE)
N_OUT = N_AB + KT
N_FFN = N_OUT + KT
PARTS = [16, 16, 12]
N_ALL = N_FFN + sum(2 * n + KT for n in PARTS)
R_HG, R_OUT, R_FFN = N_A, N_A + 4 * HEADS, N_A + 4 * HEADS + KT

STACK_GATES = [((), (8,), (9,), ())] + [((b, b + 1, b + 2), (b + 3,), (b + 4,), (b + 5,)) for b in (10, 16, 22)]

BR = (1, 2, 0)


def columns(*parts):
    at, out = 0, {}
    for name, n in parts:
        out[name] = slice(at, at + n)
        at += n
    return out, at


CP, CP_N = columns(("ident", P), ("mean_d", P), ("mean_h", P), ("seg", T), ("causal_p", P), ("causal_s", SMP),
                   ("chunk_p", 8), ("chunk_s", 8))
CA, CA_N = columns(("bias_p", HEADS * 2 * P), ("bias_pc", 2 * HEADS * NCMP), ("bias_s", 4 * T), ("bias_sc", 4 * NCMP),
                   ("pick", 2 * P), ("head", 12), ("valid", 6))
PR, PR_N = columns(("ln", 4 * KT), ("lb", 16), ("hgn", 1), ("conv", 4 * 2 * FT))


class Count:

    def __init__(self, eng, sem):
        self.eng, self.sem, self.n, self.local = eng, sem, 0, 0

    def add(self, ins):
        ins.then_inc(self.sem, 1)
        self.n = self.n + 1
        self.local += 1

    def sync(self):
        self.eng.wait_ge(self.sem, self.n)

    @contextmanager
    def loop(self, times, per):
        start = self.n
        with self.eng.Fori(0, times) as i:
            self.n, self.local = i * per + start, 0
            yield i
            assert self.local == per, f"a turn counts {self.local}, not {per}"
        self.n = start + times * per


def turns(eng, times, turn, count=None):
    start = count.n if count else 0
    turn(0)
    per = count.n - start if count else 0
    if times == 2:
        turn(1)
        return
    with eng.Fori(1, times) as j:
        if count:
            count.n = j * per + start
        turn(j)
    if count:
        count.n = start + times * per


def later(n):
    return not (isinstance(n, int) and n == 0)


def layer(nc, a, o, xt_dram, gate_dram):
    BASE, LIMIT = 16512, 229344
    slab = nc.alloc_sbuf_tensor("slab", [P, LIMIT - BASE], mybir.dt.uint8)

    class Region:
        def __init__(self, at, limit=LIMIT - BASE):
            self.at, self.limit = at, limit

        def __call__(self, name, shape, dt=F32):
            size = 4
            for s in shape[1:]:
                size *= s
            where = self.at
            self.at += (size + 31) // 32 * 32
            assert self.at <= self.limit, (name, self.at - self.limit)
            return nc.alloc_sbuf_tensor_at(name, shape, dt, offset=BASE + where)

    pers = Region(0)
    cst = pers("cst", [P, CP_N])
    prm = pers("prm", [P, PR_N])
    lbx = pers("lbx", [P, 6, 8])
    ckT = pers("ckT", [P, NCMP])
    cv = pers("cv", [P, P])
    hid = pers("hid", [P, 2, NCMP])
    gates = pers("gates", [P, 3, 24])
    gate_p = pers("gate_p", [P, 2, 24])
    gate_s = pers("gate_s", [P, 4, 3])
    gtmp = pers("gtmp", [P, 4, 12])
    stat = pers("stat", [P, 8])
    sums = pers("sums", [P, 2, 4])
    nmax = pers("nmax", [P, 2, 4])
    wgt = pers("wgt", [P, 2, 4])
    ptab = pers("ptab", [P, 16], I32)
    ring = Region(pers.at)
    raw = ring("raw", [P, 2, 16, P])
    whi = ring("whi", [P, 2, 16, P], F32R)
    wlo = ring("wlo", [P, 2, 16, P], F32R)
    H = Region(ring.at)
    h_at = ring.at
    hH = H("hH", [P, KT, T], F32R)
    hL = H("hL", [P, KT, T], F32R)
    O = Region(H.at)
    o_at = H.at
    oH = O("oH", [P, KT, T], F32R)
    oL = O("oL", [P, KT, T], F32R)
    s_at = O.at

    r = Region(s_at)
    xtok = r("xtok", [P, 3, D])
    xT0 = r("xT0", [P, KT, T])
    hf = r("hf", [P, KT, T])
    r = Region(o_at, s_at)
    junk = r("junk", [P, D])
    rows = r("rows", [P, P])
    crow = r("crow", [2 * FT, 4, P])
    rsb0 = r("rsb0", [P, T])
    r = Region(s_at)
    cat = r("cat", [P, CA_N])
    kvq_at = r.at
    kvq = r("kvq", [P, N_A, T])
    kvtok = r("kvtok", [P, 3, 12 * P])
    late_at = r.at
    prob = r("prob", [P, 2 * (512 + NCMP)])
    mgate = r("mgate", [P, 2, T])
    KTs = Region(s_at, s_at + HEADS * 2 * P * 4)("KTs", [P, 8, P])
    r = Region(late_at)
    page = r("page", [P, 4, 512])
    w2 = r("w2", [P, 2, P])
    r = Region(o_at, s_at)
    kcT = r("kcT", [P, 4, NSEQ, PAST])
    pe4 = r("pe4", [P, 4, P])
    hsg = r("hsg", [P, 2, NCMP])
    pe_row = r("pe_row", [BLK, 2, P])
    half = 8 * T * 4
    r = Region(o_at + half, o_at + 2 * half)
    kv_sel = r("kv_sel", [P, 4, 4, P])
    pT0 = r("pT0", [P, 4, P])
    r = Region(o_at + 3 * half, o_at + 4 * half)
    kv_win = r("kv_win", [P, 4, 4, P])
    pT1 = r("pT1", [P, 4, P])
    pT = [pT0, pT1]
    r = Region(kvq_at, kvq_at + 4 * T * 4)
    pTs = r("pTs", [P, 7, P])
    pTc = r("pTc", [P, 2, P])
    r = Region(kvq_at + 6 * T * 4, kvq_at + 8 * T * 4)
    qst = r("qst", [P, 2, SEQ])
    qs = Region(kvq_at + 10 * T * 4, kvq_at + 12 * T * 4)("qs", [P, 4, P])
    r = Region(s_at)
    kinv = r("kinv", [P, 2, T])
    kend = r("kend", [P, 2, T])
    qdec = r("qdec", [P, 2, T])
    ogs = r("ogs", [P, 2, T])
    cum = r("cum", [P, 2, T])
    vT = r("vT", [P, 2, T])
    fsig = r("fsig", [P, T])
    nsig = r("nsig", [P, T])
    fmul = r("fmul", [P, T])
    fset = r("fset", [P, T])
    osig = r("osig", [P, T])
    kend_tok = r("kend_tok", [P, 3, P])
    v_tok = r("v_tok", [P, 3, P])
    vmask = r("vmask", [P, 3, 8, P])
    att = r("att", [P, T])
    st = r("st", [P, 16, P])
    sfin = r("sfin", [P, 2, P])
    s0 = r("s0", [P, 2, DB, P])
    sn = r("sn", [P, 2, DB, P])
    osb = r("osb", [P, T])
    osq = r("osq", [P, T])
    orn = r("orn", [P, T])
    r = Region(s_at)
    mH = r("mH", [P, KT, T], F32R)
    mL = r("mL", [P, KT, T], F32R)
    ffn_at = r.at
    sg = r("sg", [P, 2, 2, T])
    mix = r("mix", [P, 2, T])
    mix2 = r("mix2", [P, 2, T])
    r = Region(ffn_at)
    y1 = r("y1", [P, KT, T])
    hist = r("hist", [P, 2 * FT, 2 * DB])
    sq = r("sq", [P, 2, T])
    sqs = r("sqs", [P, T])
    rsb = r("rsb", [P, T])
    x1 = Region(o_at)("x1", [P, KT, T])
    acc = Region(o_at + KT * T * 4)("acc", [P, KT, T])
    hrow = Region(o_at + KT * T * 4)("hrow", [2 * FT, 2 * DB, P])
    r = Region(s_at)
    aH = r("aH", [P, KT, T], F32R)
    aL = r("aL", [P, KT, T], F32R)
    ue = r("ue", [P, 2, 2, UW])
    cc = r("cc", [P, 2, UW - 2])
    gg = r("gg", [P, T])
    newc = r("newc", [P, 2 * FT, 2 * NSEQ])
    assert r.at <= ffn_at + KT * T * 4
    r = Region(h_at, o_at)
    ytok = r("ytok", [P, 3, D])
    crow_out = r("crow_out", [2 * FT, 2 * NSEQ, P])

    ps = nc.alloc_psum_tensor("ps", [P, 8, 512], F32)

    def c_(name):
        return cst[:, CP[name]]

    ident = c_("ident")
    cat_ = {k: cat[:, v] for k, v in CA.items()}
    bias_p = cat_["bias_p"].rearrange("p (h k) -> p h k", h=HEADS)
    bias_pc = cat_["bias_pc"].rearrange("p (t h k) -> p t h k", t=2, h=HEADS)
    bias_s = cat_["bias_s"].rearrange("p (t k) -> p t k", t=4)
    bias_sc = cat_["bias_sc"].rearrange("p (t k) -> p t k", t=4)
    pick = cat_["pick"].rearrange("p (t k) -> p t k", t=2)
    ln = prm[:, PR["ln"]].rearrange("p (n k) -> p n k", n=4)
    conv = prm[:, PR["conv"]].rearrange("p (n k) -> p n k", n=4)
    hgn = prm[:, PR["hgn"]]

    S = nc.alloc_semaphore
    x_in, cst_in, rows_in, cat_in, w2_in, hrow_in, x1_in, xt_out = map(
        S, ("x_in", "cst_in", "rows_in", "cat_in", "w2_in", "hrow_in", "x1_in", "xt_out"))
    loaded = [S("loaded0"), S("loaded1")]
    ab_loaded = [S("ab_loaded0"), S("ab_loaded1")]
    hi_ready, lo_ready = S("hi_ready"), S("lo_ready")
    used = S("used")
    free = [S("free0"), S("free1")]
    dv_c, ac_c, po_c = S("dv_c"), S("ac_c"), S("po_c")
    par_ps, par_ok, ssq_ok, rms_v, rs_ok, rsb_ps, rsb_ok = map(
        S, ("par_ps", "par_ok", "ssq_ok", "rms_v", "rs_ok", "rsb_ps", "rsb_ok"))
    xt_ps, xt_ok, hf_ok, hh_ok, hl_ok = map(S, ("xt_ps", "xt_ok", "hf_ok", "hh_ok", "hl_ok"))
    tok_ps, tok_ok, kv_out = S("tok_ps"), S("tok_ok"), S("kv_out")
    ptab_in = S("ptab_in")
    page_in = [S(f"page_in{i}") for i in range(4)]
    pe_in, pe_ok, page_ps, page_ok = S("pe_in"), S("pe_ok"), S("page_ps"), S("page_ok")
    hid_sg, hid_ok, cc_ps, cc_ok = S("hid_sg"), S("hid_ok"), S("cc_ps"), S("cc_ok")
    gate_f, gate_t = S("gate_f"), S("gate_t")
    gate_ok, gsel_ps, gsel_ok = S("gate_ok"), S("gsel_ps"), S("gsel_ok")
    q_ok, sc_ps, sc_rd, nm_ok, ex_ok, pn_ok = (S(n) for n in ("q_ok", "sc_ps", "sc_rd", "nm_ok", "ex_ok", "pn_ok"))
    pt_ps, pt_ok, ov_ps, oh_ok, ol_ok = (S(n) for n in ("pt_ps", "pt_ok", "ov_ps", "oh_ok", "ol_ok"))
    sel_in, win_in = S("sel_in"), S("win_in")
    kt_ps, kt_ok, ks_ps = S("kt_ps"), S("kt_ok"), S("ks_ps")
    f_sig, v_ok, q_rd, o_sig, f_done, og_ok = (S(n) for n in ("f_sig", "v_ok", "q_rd", "o_sig", "f_done", "og_ok"))
    t_ps, t_ok, m_ok, u_ps, s_ok, ho_ps, ho_sb, hm_ps, hv_ok, hr_ok, hn_ok, hoh, hol = (
        S(n) for n in ("t_ps", "t_ok", "m_ok", "u_ps", "s_ok", "ho_ps", "ho_sb", "hm_ps", "hv_ok", "hr_ok", "hn_ok",
                       "hoh", "hol"))
    s0_in = [S("s0_in0"), S("s0_in1")]
    st_out = [S("st_out0"), S("st_out1")]
    stat_zero, hist_ps, hist_ok = S("stat_zero"), S("hist_ps"), S("hist_ok")
    mg_rd = [S("mg_rd0"), S("mg_rd1")]
    mg_mix, mg_hi, mg_lo = S("mg_mix"), S("mg_hi"), S("mg_lo")
    gs_rd = [S("gs_rd0"), S("gs_rd1")]
    spilled = [S("spilled0"), S("spilled1")]
    sg_in = [S("sg_in0"), S("sg_in1")]
    y_sq, y_add, mean_ps, mean_v, rstd_ok = S("y_sq"), S("y_add"), S("mean_ps"), S("mean_v"), S("rstd_ok")
    x_new, x_sq, x_add, h_new = S("x_new"), S("x_sq"), S("x_add"), S("h_new")
    h2h, h2l = S("h2h"), S("h2l")
    u_hist, u_ev, c_ok, g_ok, m_new, a_hi, a_lo, newc_ok = (
        S(n) for n in ("u_hist", "u_ev", "c_ok", "g_ok", "m_new", "a_hi", "a_lo", "newc_ok"))
    d_acc, d_sq, d_add = S("d_acc"), S("d_sq"), S("d_add")
    y_fin, yt_ps, yt_ok, nc_ps, nc_ok, y_out, copy_out = (
        S(n) for n in ("y_fin", "yt_ps", "yt_ok", "nc_ps", "nc_ok", "y_out", "copy_out"))

    w_in = a["w_in"][0]
    HGCOL = [COL_HF, COL_HI, COL_HQ, COL_HO]

    def tile_src(w, rows, at, step=0):
        if isinstance(step, int):
            return w[rows, at + step:at + step + P].rearrange("(k p) n -> p k n", p=P)
        return w[rows, at:][:, ds(step, P)].rearrange("(k p) n -> p k n", p=P)

    block = ctx_block = nc.Block()
    with block:
        @block.sync
        def _(sp):
            sp.dma_start(xtok[:, 0, :], a["x_prompt"][0, 0:P, :]).then_inc(x_in, 16)
            sp.dma_start(xtok[:, 1, :], a["x_prompt"][0, P:SEQ, :]).then_inc(x_in, 16)
            sp.dma_start(xtok[0:SMP, 2, :], a["x_sample"].rearrange("b s d -> (b s) d")).then_inc(x_in, 16)

            def load(n, slot, src, kn=16, first=False, direct=False):
                if not first:
                    sp.wait_ge(lo_ready, n - 1)
                    if direct:
                        sp.wait_ge(used, n - 1)
                sp.dma_start(raw[:, slot, 0:kn, :], src).then_inc(loaded[slot], 16)

            for u in range(2):
                load(u, u, tile_src(w_in, slice(0, D), COL_KV + u * P), first=True)
            with sp.Fori(0, 5) as j:
                for u in range(2):
                    load(j * 2 + (2 + u), u, tile_src(w_in, slice(0, D), COL_KV + (2 + u) * P, j * 256))
            with sp.Fori(0, 4) as j:
                for u in range(2):
                    load(j * 2 + (12 + u), u, tile_src(w_in, slice(0, D), u * P, j * 256))
            load(N_GATE, N_GATE % 2, tile_src(w_in, slice(0, D), COL_GATE))
            for c in range(2):
                for q in range(4):
                    n = N_CMP + 4 * c + q
                    load(n, n % 2, a["cmp_w1"][0, 16 * q:16 * q + 16, c].rearrange("l d e -> d l e"), direct=True)
            def merge_gate(m, par, n, direct=False):
                load(n, (N_MG + par) % 2, tile_src(w_in, slice(0, D), COL_MRG + par * D, m * P), direct=direct)

            for par in range(2):
                merge_gate(0, par, N_MG + par, direct=True)
            with sp.Fori(1, M_LATE) as m:
                for par in range(2):
                    merge_gate(m, par, m * 2 + (N_MG + par))
            for u in range(4):
                load(N_HG + u, (N_HG + u) % 2, tile_src(w_in, slice(0, D), HGCOL[u]))
            with sp.Fori(0, HEADS - 1) as h:
                for u in range(4):
                    load(h * 4 + (N_HG + 4 + u), (N_HG + u) % 2, tile_src(w_in, slice(0, D), HGCOL[u] + P, h * P))
            def branch_src(name, m):
                return a[name][0].rearrange("(k p) (m n) -> m p k n", p=P, n=P)[ds(m, 1)].rearrange(
                    "o p k n -> (o p) k n")

            for m in range(M_LATE, KT):
                for par in range(2):
                    merge_gate(m, par, N_MG2 + 2 * (m - M_LATE) + par)
            with sp.Fori(0, KT // 2) as j:
                for v in range(2):
                    slot = (N_AB + v) % 2
                    load(j * 2 + (N_AB + v), slot, branch_src("w_branch_a", j * 2 + v), kn=8)
                    sp.dma_start(raw[:, slot, 8:16, :], branch_src("w_branch_b", j * 2 + v)
                                 ).then_inc(ab_loaded[slot], 16)
            with sp.Fori(0, KT // 2) as j:
                for u in range(2):
                    load(j * 2 + (N_OUT + u), (N_OUT + u) % 2,
                         tile_src(a["w_out"][0], slice(0, D), u * P, j * 256))
            n0, t0 = N_FFN, 0
            for cnt in PARTS:
                with sp.Fori(0, cnt) as i:
                    for u in range(2):
                        load(i * 2 + (n0 + u), (n0 + u) % 2,
                             tile_src(a["w_up"][0], slice(0, D), u * DFF + t0 * P, i * P))
                n0 += 2 * cnt
                with sp.Fori(0, KT // 2) as j:
                    for u in range(2):
                        load(j * 2 + (n0 + u), (n0 + u) % 2,
                             tile_src(a["w_down"][0], slice(t0 * P, (t0 + cnt) * P), u * P, j * 256), kn=cnt)
                n0 += KT
                t0 += cnt

        @block.gpsimd
        def _(po):
            po.dma_start(ptab[0:1, :], a["page_table"].rearrange("(o b) n -> o (b n)", o=1)).then_inc(ptab_in, 16)
            po.dma_start(pe_row[:], a["cmp_pe"][0]).then_inc(pe_in, 16)
            po.wait_ge(x_in, 48)
            po.wait_ge(xt_ok, KT)
            po.dma_start(xt_dram.rearrange("p (k t) -> p k t", k=KT), xT0[:]).then_inc(xt_out, 16)
            win = a["state_win_kv"][0].rearrange("b w c g d -> b (w c g d)")
            po.dma_start(o[7][0].rearrange("b w c g d -> b (w c g d)")[:, 0:(PAST - DS) * 512],
                         win[:, DS * 512:PAST * 512]).then_inc(copy_out, 16)
            po.wait_ge(ptab_in, 16)
            po.wait_ge(hh_ok, KT)
            po.wait_ge(hl_ok, KT)
            po.dma_start(w2[:], a["cmp_w2"][0].rearrange("c e f -> e c f")).then_inc(w2_in, 16)
            cmp_pages = a["cache_cmp_kv"][0].rearrange("n t c g d -> n t (c g d)")
            sel_pages = a["cache_sel_kv"][0]

            def cmp_page(i, slot):
                idx = po.value_load(ptab[0:1, ds(i, 1)] if not isinstance(i, int) else ptab[0:1, i:i + 1],
                                    min_val=0, max_val=N_PHYS - 1)
                po.dma_start(page[:, slot, :], cmp_pages[ds(idx, 1)].rearrange("o t c -> (o t) c")
                             ).then_inc(page_in[slot], 16)

            for i in range(4):
                cmp_page(i, i)
            with po.Fori(0, 3) as j:
                for u in range(4):
                    po.wait_ge(page_ps, j * 4 + (u + 1))
                    cmp_page(j * 4 + (4 + u), u)
            po.dma_start(cat[:], a["att_const"]).then_inc(cat_in, 16)
            po.wait_ge(tok_ok, 12)
            for n, name in enumerate((2, 4, 6)):
                cols = slice(512 * n, 512 * n + 512)
                po.dma_start(o[name][0, 0].rearrange("(a p) c g d -> p a (c g d)", p=P),
                             kvtok[:, 0:2, cols]).then_inc(kv_out, 16)
            for n, name in enumerate((3, 5)):
                po.dma_start(o[name][0].rearrange("b s c g d -> (b s) (c g d)"),
                             kvtok[0:SMP, 2, 512 * n:512 * n + 512]).then_inc(kv_out, 16)
            for b in range(DB):
                po.dma_start(o[7][0, b, PAST - DS:PAST].rearrange("s c g d -> s (c g d)"),
                             kvtok[b * DS:b * DS + DS, 2, 1024:1536]).then_inc(kv_out, 16)
            po.wait_ge(hid_ok, 2)
            for k in range(4):
                g, bh = k // 2, k % 2
                if k:
                    po.wait_ge(ov_ps, HEADS + k)
                for j in range(4):
                    for t in range(2):
                        i = (4 * bh + j) * 2 + t
                        idx = po.value_load(ptab[0:1, i:i + 1], min_val=0, max_val=N_PHYS - 1)
                        po.dma_start(kv_sel[:, j, 2 * t:2 * t + 2, :],
                                     sel_pages[ds(idx, 1), :, :, g, :].rearrange("o t c d -> (o t) c d")
                                     ).then_inc(sel_in, 16)
                for j in range(4):
                    for t in range(2):
                        po.dma_start(kv_win[:, j, 2 * t:2 * t + 2, :],
                                     a["state_win_kv"][0, 4 * bh + j, t * PAGE:(t + 1) * PAGE, :, g, :]
                                     ).then_inc(win_in, 16)
            po.wait_ge(ol_ok, HEADS + 4)
            st_in = a["state_hgrn"][0].rearrange("b h k v -> h k b v")
            sp_out = o[8][0, 0]
            ss_out = o[9][0].rearrange("b h k v -> h k b v")

            def state_in(h, par):
                src = st_in[ds(h, 1)].rearrange("o k b v -> (o k) b v")
                po.dma_start(s0[:, par], src).then_inc(s0_in[par], 16)

            def state_out(h, par):
                po.wait_ge(s_ok, h + 1)
                po.dma_start(sp_out[ds(h, 1)].rearrange("o k v -> (o k) v"), sfin[:, par]).then_inc(st_out[par], 16)
                po.dma_start(ss_out[ds(h, 1)].rearrange("o k b v -> (o k) b v"), sn[:, par]).then_inc(st_out[par], 16)

            state_in(0, 0)
            state_in(1, 1)
            with po.Fori(0, HEADS // 2 - 1) as j:
                for par in range(2):
                    state_out(j * 2 + par, par)
                    po.wait_ge(ho_ps, j * 2 + (par + 1))
                    state_in(j * 2 + (par + 2), par)
            for par in range(2):
                state_out(HEADS - 2 + par, par)
            for par in range(2):
                po.wait_ge(st_out[par], 16 * HEADS)
                po.wait_ge(spilled[par], 16 * KT)
            po.wait_ge(hol, HEADS)

            def gates_in(m, v):
                po.dma_start(sg[:, v], gate_dram[ds(m, 1)].rearrange("o s p t -> p (o s) t")).then_inc(sg_in[v], 16)

            gates_in(0, 0)
            gates_in(1, 1)
            with po.Fori(0, KT // 2 - 1) as j:
                for v in range(2):
                    po.wait_ge(mg_rd[v], j + 1)
                    gates_in(j * 2 + (2 + v), v)
            po.wait_ge(mg_lo, KT)
            po.wait_ge(used, N_OUT)
            po.wait_ge(xt_out, 16)
            po.dma_start(x1[:], xt_dram.rearrange("p (k t) -> p k t", k=KT)).then_inc(x1_in, 16)
            po.dma_start(hrow[:], a["state_conv"][0].rearrange("b j (f p) -> f (b j) p", p=P)).then_inc(hrow_in, 16)
            po.wait_ge(nc_ok, 5)
            po.dma_start(o[10][0, 0].rearrange("j (f p) -> f j p", p=P), crow_out[:, 0:2, :]).then_inc(y_out, 16)
            po.dma_start(o[11][0].rearrange("b j (f p) -> f (b j) p", p=P), crow_out[:, 2:, :]).then_inc(y_out, 16)
            for q in range(4):
                po.wait_ge(yt_ok, 4 * q + 4)
                cols = slice(512 * q, 512 * q + 512)
                po.dma_start(o[0][0].rearrange("(a p) d -> p a d", p=P)[:, :, cols], ytok[:, 0:2, cols]
                             ).then_inc(y_out, 16)
                po.dma_start(o[1].rearrange("b s d -> (b s) d")[:, cols], ytok[0:SMP, 2, cols]).then_inc(y_out, 16)
            po.wait_ge(copy_out, 16)
            po.wait_ge(kv_out, 16 * 13)
            for par in range(2):
                po.wait_ge(st_out[par], 16 * HEADS)
            po.wait_ge(y_out, 16 * 10)

        @block.scalar
        def _(act):
            A = Count(act, ac_c)

            def split(n, half, slot, ab=None):
                act.wait_ge(loaded[slot], half * 16 + 16)
                if ab is not None:
                    act.wait_ge(ab_loaded[slot], ab * 16 + 16)
                if not isinstance(n, int) or n >= 2:
                    act.wait_ge(used, n - 1)
                act.activation(whi[:, slot], raw[:, slot], ACT.Copy).then_inc(hi_ready, 1)

            def split_after(n, i=None, per=0):
                if n + 2 < N_ALL:
                    m = n + 2
                    if i is None:
                        split(m, m // 2, m % 2, (m - N_AB) // 2 if N_AB <= m < N_OUT else None)
                    else:
                        split(i * per + m, i * (per // 2) + m // 2, m % 2)

            act.dma_start(cst[:], a["const"]).then_inc(cst_in, 16)
            for n, name in enumerate(("ln_mix_pre", "ln_mix_post", "ln_ffn_pre", "ln_ffn_post")):
                act.dma_start(rows[KT * n:KT * n + KT, :], a[name][0].rearrange("(k p) -> k p", p=P)
                              ).then_inc(rows_in, 16)
            act.dma_start(rows[64:80, :], a["hg_lb_raw"].rearrange("r (k p) -> (r k) p", p=P)).then_inc(rows_in, 16)
            act.dma_start(rows[80:81, :], a["hg_norm_w"]).then_inc(rows_in, 16)
            act.dma_start(crow[:, 0:3, :], a["conv_w"][0].rearrange("j (f p) -> f j p", p=P)).then_inc(rows_in, 16)
            act.dma_start(crow[:, 3, :], a["conv_b"][0].rearrange("(f p) -> f p", p=P)).then_inc(rows_in, 16)
            act.wait_ge(x_in, 48)
            act.wait_ge(stat_zero, 1)
            for i in range(3):
                m = P if i < 2 else SMP
                if i:
                    A.sync()
                ins = act.activation(junk[0:m, :], xtok[0:m, i, :], ACT.Square, accum_out=stat[0:m, i:i + 1])
                if i < 2:
                    A.add(ins)
                else:
                    ins.then_inc(ssq_ok, 1)
            act.wait_ge(rms_v, 1)
            act.activation(stat[:, 3:6], stat[:, 3:6], ACT.Sqrt).then_inc(rs_ok, 1)
            for k in range(KT):
                act.wait_ge(xt_ps, k + 1)
                act.activation(xT0[:, k, :], ps[:, 2 + k % 6, 0:T], ACT.Copy).then_inc(xt_ok, 1)
            act.wait_ge(par_ps, 1)
            act.activation(prm[:], ps[:, 1, 0:PR_N], ACT.Copy).then_inc(par_ok, 1)
            act.wait_ge(rsb_ps, 1)
            act.activation(rsb0[:], ps[:, 0, 0:T], ACT.Copy).then_inc(rsb_ok, 1)
            for r_ in range(2):
                for g in range(2):
                    ins = act.activation(pe4[:].rearrange("p (c g) (r l) -> p c g r l", c=2, r=2)[:, :, g, r_, :],
                                         ps[:, 0, T:T + P].rearrange("p (c l) -> p c l", c=2), ACT.Copy)
            ins.then_inc(pe_ok, 1)
            act.wait_ge(rms_v, 2)
            act.activation(lbx[:, 2:4, :], lbx[:, 0:2, :], ACT.Exp).then_inc(rs_ok, 1)
            split(0, 0, 0)
            split(1, 0, 1)
            for k in range(KT):
                act.wait_ge(hf_ok, k + 1)
                act.activation(hH[:, k, :], hf[:, k, :], ACT.Copy).then_inc(hh_ok, 1)
            act.wait_ge(xt_out, 16)
            def evacuate(n, u, i=None):
                split_after(u, i, 4)
                act.wait_ge(used, n + 1)
                act.activation(kvq[:, ds(n, 1), :], ps[:, u % 2:u % 2 + 1, 0:T], ACT.Copy).then_inc(free[u % 2], 1)

            for n in range(4):
                evacuate(n, n)

            def turn(j):
                for u in range(4):
                    evacuate(j * 4 + (4 + u), 4 + u, j)

            turns(act, N_A // 4 - 1, turn)
            act.wait_ge(page_ps, 2 * DB)
            act.wait_ge(used, N_GATE + 1)
            act.activation(mgate[0:24, 0, :], ps[0:24, 2, 0:T], ACT.Sigmoid).then_inc(gate_f, 1)
            split_after(N_GATE)
            act.wait_ge(gate_t, 1)
            act.activation(gates[:], ps[:, 2, 0:72].rearrange("p (a b) -> p a b", a=3), ACT.Copy
                           ).then_inc(gate_ok, 1)
            for c in range(2):
                for q in range(4):
                    split_after(N_CMP + 4 * c + q)
                act.wait_ge(used, N_CMP + 4 * c + 4)
                act.activation(hsg[:, c, :], ps[:, c, 0:NCMP], ACT.Sigmoid).then_inc(hid_sg, 1)
            for f in range(12):
                act.wait_ge(tok_ps, f + 1)
                b = 4 + f % 4
                A.add(act.activation(kvtok[:, 0:2, f * P:f * P + P],
                                     ps[:, b, 0:256].rearrange("p (a d) -> p a d", a=2), ACT.Copy))
                act.activation(kvtok[0:SMP, 2, f * P:f * P + P], ps[0:SMP, b, 256:384], ACT.Copy
                               ).then_inc(tok_ok, 1)
                if f == 3:
                    act.wait_ge(cc_ps, 1)
                    act.activation(ckT[:], ps[:, 2, 0:NCMP], ACT.Copy).then_inc(cc_ok, 1)
                    act.activation(cv[0:NCMP, :], ps[0:NCMP, 3, 0:P], ACT.Copy).then_inc(cc_ok, 1)

            def gate_step(par, m, n=N_MG, bank=None):
                act.wait_ge(used, m * 2 + (n + par + 1))
                if later(m):
                    act.wait_ge(spilled[par], m * 16)
                act.activation(mgate[:, par, :], ps[:, 1 + 4 * par if bank is None else bank, 0:T], ACT.Sigmoid
                               ).then_inc(gs_rd[par], 1)
                act.wait_ge(gs_rd[par], m + 1)
                act.dma_start(gate_dram[ds(m, 1), par].rearrange("o p t -> (o p) t"), mgate[:, par, :]
                              ).then_inc(spilled[par], 16)
                if isinstance(m, int):
                    split_after(m * 2 + n + par)
                else:
                    c = n + par + 2
                    split(m * 2 + c, m + c // 2, c % 2)

            def exps(u, par, nk, width):
                act.wait_ge(nm_ok, u + 1)
                for b in range(3):
                    w = slice(b * width, b * width + nk) if b < 2 else slice(2 * width, 2 * width + NCMP)
                    base = par
                    ins = act.activation(prob[:, base + w.start:base + w.stop], prob[:, base + w.start:base + w.stop],
                                         ACT.Exp, bias=nmax[:, (1 if base else 0), BR[b]:BR[b] + 1],
                                         accum_out=sums[:, (1 if base else 0), BR[b]:BR[b] + 1])
                    if b == 2:
                        ins.then_inc(ex_ok, 1)
                    else:
                        A.add(ins)

            PW = 512 + NCMP
            for g in range(GROUPS):
                def turn(t):
                    if later(t * 4 + 8 * g):
                        act.wait_ge(sc_ps, t * 4 + 8 * g)
                    for par in range(2):
                        act.activation(qst[:, par, :],
                                       kvq[:, ds(t * 2 + (12 + 4 * g + par), 1), 0:SEQ].rearrange("p o t -> p (o t)"),
                                       ACT.Copy, scale=SCALE).then_inc(q_ok, 1)
                    for par in range(2):
                        h = t * 2 + (4 * g + par)
                        for qt in range(2):
                            exps(h * 2 + qt, qt * PW, (qt + 1) * P, (qt + 1) * P)
                        for qt in range(2):
                            act.wait_ge(pt_ps, h * 2 + (qt + 1))
                            if later(h):
                                act.wait_ge(ov_ps, h)
                            A.add(act.activation(pT[qt][:, 0:2 * (qt + 1), :],
                                                 ps[:, 6, 0:256 * (qt + 1)].rearrange("p (a d) -> p a d", d=P), ACT.Copy))
                            act.activation(pTc[0:NCMP, qt, :], ps[0:NCMP, 7, 0:P], ACT.Copy).then_inc(pt_ok, 1)
                        gate_step(par, t + 2 * g)
                        act.wait_ge(ov_ps, h + 1)
                        act.activation(oH[:, ds(h, 1), 0:SEQ], ps[:, 0:1, 0:SEQ], ACT.Copy).then_inc(oh_ok, 1)
                turns(act, HPG // 2, turn, A)
            for k in range(4):
                g, bh = k // 2, k % 2
                for h4 in range(4):
                    ins = act.activation(
                        qs[:, k, :].rearrange("p (j h s) -> p j h s", j=4, h=4)[:, :, h4, :],
                        kvq[:, 12 + 4 * g + h4, SEQ + 32 * bh:SEQ + 32 * bh + 32].rearrange("p (j s) -> p j s", j=4),
                        ACT.Copy, scale=SCALE)
                ins.then_inc(q_ok, 1)
            act.wait_ge(sc_rd, 2 * HEADS)
            for k in range(4):
                g, bh = k // 2, k % 2
                u = 16 + k
                gates_at = STACK_GATES[k]
                for i in gates_at[0]:
                    gate_step(i % 2, i // 2)
                for br in range(2):
                    act.wait_ge(kt_ps, 2 * k + br + 1)
                    if br or k:
                        act.wait_ge(ks_ps, 2 * k + br)
                    A.add(act.activation(KTs[:, 0:4, :], ps[:, 6, :].rearrange("p (a d) -> p a d", a=4), ACT.Copy))
                    act.activation(KTs[:, 4:8, :], ps[:, 7, :].rearrange("p (a d) -> p a d", a=4), ACT.Copy
                                   ).then_inc(kt_ok, 1)
                    for i in gates_at[1 + br]:
                        gate_step(i % 2, i // 2)
                exps(u, 0, T, T)
                act.wait_ge(pt_ps, u + 1)
                A.add(act.activation(pTs[:, 0:2, :], ps[:, 6, 0:256].rearrange("p (a d) -> p a d", a=2), ACT.Copy))
                A.add(act.activation(pTs[0:SMP, 2, :], ps[0:SMP, 6, 256:384], ACT.Copy))
                A.add(act.activation(pTs[:, 3:5, :], ps[:, 7, 0:256].rearrange("p (a d) -> p a d", a=2), ACT.Copy))
                A.add(act.activation(pTs[0:SMP, 5, :], ps[0:SMP, 7, 256:384], ACT.Copy))
                act.activation(pTs[0:NCMP, 6, :], ps[0:NCMP, 7, 384:512], ACT.Copy).then_inc(pt_ok, 1)
                for i in gates_at[3]:
                    gate_step(i % 2, i // 2)
                act.wait_ge(ov_ps, HEADS + k + 1)
                act.activation(
                    oH[:, 4 * g:4 * g + 4, SEQ + 32 * bh:SEQ + 32 * bh + 32].rearrange("p h (j s) -> p h j s", j=4),
                    ps[:, 0, 0:P].rearrange("p (j h s) -> p h j s", j=4, h=4), ACT.Copy).then_inc(oh_ok, 1)

            def tail1(h):
                act.wait_ge(t_ps, h + 1)
                A.add(act.activation(kend_tok[:, 0:2, :], ps[:, 2, 0:256].rearrange("p (a d) -> p a d", a=2), ACT.Copy))
                A.add(act.activation(kend_tok[0:SMP, 2, :], ps[0:SMP, 2, 256:384], ACT.Copy))
                A.add(act.activation(v_tok[:, 0:2, :], ps[:, 3, 0:256].rearrange("p (a d) -> p a d", a=2), ACT.Copy))
                act.activation(v_tok[0:SMP, 2, :], ps[0:SMP, 3, 256:384], ACT.Copy).then_inc(t_ok, 1)

            def tail2(h):
                act.wait_ge(ho_ps, h + 1)
                if later(h):
                    act.wait_ge(hol, h)
                A.add(act.activation(osq[:], ps[:, 5, 0:T], ACT.Square))
                act.activation(osb[:], ps[:, 5, 0:T], ACT.Copy).then_inc(ho_sb, 1)

            def tail3(h):
                act.wait_ge(hv_ok, h + 1)
                act.activation(orn[:], orn[:], ACT.Sqrt).then_inc(hr_ok, 1)
                act.wait_ge(hn_ok, h + 1)
                act.activation(oH[:, ds(h + 8, 1), :], osb[:].rearrange("p (o t) -> p o t", o=1), ACT.Copy
                               ).then_inc(hoh, 1)

            def window(h, par, i=None, k=0):
                n = N_HG + 4 * k
                nn = n if i is None else i * 8 + n
                if k:
                    tail1(h - 1)
                split_after(n, i, 8)
                act.wait_ge(used, nn + 1)
                if later(h):
                    act.wait_ge(f_done, h)
                A.add(act.activation(fsig[:], ps[:, 0, 0:T], ACT.Sigmoid))
                act.activation(nsig[:], ps[:, 0, 0:T], ACT.Sigmoid, scale=-1.0).then_inc(free[0], 1)
                split_after(n + 1, i, 8)
                act.wait_ge(used, nn + 2)
                act.activation(vT[:, par, :], ps[:, 1, 0:T], ACT.Copy).then_inc(free[1], 1)
                if k:
                    tail2(h - 1)
                split_after(n + 2, i, 8)
                if k:
                    tail3(h - 1)
                split_after(n + 3, i, 8)
                act.wait_ge(used, nn + 4)
                act.wait_ge(free[1], h * 2 + R_HG // 2)
                act.activation(osig[:], ps[:, 1, 0:T], ACT.Sigmoid).then_inc(o_sig, 1)

            act.wait_ge(kv_out, 16 * 13)
            act.wait_ge(ol_ok, HEADS + 4)
            window(0, 0)
            window(1, 1, None, 1)
            window(2, 0, None, 2)
            with A.loop(2, 10) as i:
                window(i * 2 + 3, 1, i, 3)
                window(i * 2 + 4, 0, i, 4)
            window(7, 1, None, 7)
            late = [(i % 2, M_LATE + i // 2, N_MG2 - 2 * M_LATE, i % 2) for i in range(4)]
            tail1(7)
            gate_step(*late[0])
            tail2(7)
            gate_step(*late[1])
            tail3(7)
            gate_step(*late[2])
            gate_step(*late[3])

            act.wait_ge(hol, HEADS)
            for par in range(2):
                act.wait_ge(spilled[par], 16 * KT)
            for par in range(2):
                act.wait_ge(st_out[par], 16 * HEADS)
            def merged(j, last):
                for v in range(2):
                    m, c = j * 2 + v, N_AB + v + 2
                    if last:
                        split_after(N_AB + m)
                    else:
                        split(j * 2 + c, j + c // 2, c % 2, j + 1)
                    act.wait_ge(mg_mix, m + 1)
                    act.activation(mH[:, ds(m, 1), :], mix[:, v:v + 1, :], ACT.Copy).then_inc(mg_hi, 1)

            with act.Fori(0, KT // 2 - 1) as j:
                merged(j, False)
            merged(KT // 2 - 1, True)
            def turn(j):
                for u in range(2):
                    m = j * 2 + u
                    split_after(N_OUT + u, j, 2)
                    act.wait_ge(used, m + (N_OUT + 1))
                    if later(m):
                        act.wait_ge(y_add, m)
                    act.activation(sq[:, u, :], ps[:, u, 0:T], ACT.Square).then_inc(y_sq, 1)
                    act.activation(y1[:, ds(m, 1), :].rearrange("p o t -> p (o t)"), ps[:, u, 0:T], ACT.Identity,
                                   scale=ln[:, 1, ds(m, 1)]).then_inc(free[u], 1)

            turns(act, KT//2, turn)
            act.wait_ge(mean_v, 1)
            act.activation(rsb[:], rsb[:], ACT.Sqrt).then_inc(rstd_ok, 1)
            for k in range(KT):
                act.wait_ge(x_new, k + 1)
                if k >= 2:
                    act.wait_ge(x_add, k - 1)
                act.activation(sq[:, k % 2, :], x1[:, k, :], ACT.Square).then_inc(x_sq, 1)
            act.wait_ge(mean_v, 2)
            act.activation(rsb[:], rsb[:], ACT.Sqrt).then_inc(rstd_ok, 1)
            for k in range(KT):
                act.wait_ge(h_new, k + 1)
                act.activation(hH[:, k, :], y1[:, k, :], ACT.Copy).then_inc(h2h, 1)
            for i in range(4):
                act.wait_ge(hist_ps, i + 1)
                act.activation(hist[:, :, 4 * i:4 * i + 4],
                               ps[:, 3 + i, 0:4 * 2 * FT].rearrange("p (b f) -> p f b", b=4), ACT.Copy
                               ).then_inc(hist_ok, 1)

            n0, r0, i0 = N_FFN, R_FFN, 0
            for part, cnt in enumerate(PARTS):
                def turn(j):
                    for par in range(2):
                        i = j * 2 + (i0 + par)
                        for s in range(2):
                            c = 2 * par + s
                            split_after(n0 + c, j, 4)
                            act.wait_ge(used, j * 4 + (n0 + c + 1))
                            act.wait_ge(u_hist, i * 2 + (s + 1))
                            A.add(act.activation(ue[:, par, s, 2:2 + SEQ], ps[:, s, 0:SEQ], ACT.Copy))
                            act.activation(ue[:, par, s, 2 + SEQ:UW].rearrange("p (b c) -> p b c", b=DB)[:, :, 2:],
                                           ps[:, s, SEQ:T].rearrange("p (b c) -> p b c", b=DB), ACT.Copy
                                           ).then_inc(free[s], 1)
                            A.sync()
                            act.wait_ge(free[s], j * 2 + (r0 // 2 + par + 1))
                            if later(i):
                                act.wait_ge(m_new, i)
                            col = i + s * FT
                            act.activation(cc[:, s, :], ue[:, par, s, 0:UW - 2], ACT.Identity,
                                           scale=conv[:, 0, ds(col, 1)], bias=conv[:, 3, ds(col, 1)]
                                           ).then_inc(u_ev, 1)
                        act.wait_ge(c_ok, i * 2 + 2)
                        act.activation(cc[:, 1, :], cc[:, 1, :], ACT.Gelu_apprx_tanh).then_inc(g_ok, 1)
                        act.wait_ge(m_new, i + 1)
                        act.activation(aH[:, ds(j * 2 + par, 1), :], gg[:].rearrange("p (o t) -> p o t", o=1), ACT.Copy
                                       ).then_inc(a_hi, 1)

                turns(act, cnt//2, turn, A)
                n0 += 2 * cnt
                r0 += 2 * cnt
                i0 += cnt
                if part < 2:
                    def turn(j):
                        for u in range(2):
                            split_after(n0 + u, j, 2)

                    turns(act, KT//2, turn)
                else:
                    for i in range(5):
                        w = 4 if i < 4 else 2
                        act.wait_ge(nc_ps, i + 1)
                        act.activation(crow_out[:, 4 * i:4 * i + w, :],
                                       ps[0:2 * FT, 3 + i, 0:w * P].rearrange("p (a d) -> p a d", a=w), ACT.Copy
                                       ).then_inc(nc_ok, 1)
                    act.wait_ge(x_add, KT)

                    def square(m, u, j):
                        act.wait_ge(free[u], j + (r0 // 2 + 1))
                        if later(m):
                            act.wait_ge(d_add, m)
                        act.activation(sq[:, u, :], acc[:, ds(m, 1), :].rearrange("p o t -> p (o t)"), ACT.Square
                                       ).then_inc(d_sq, 1)

                    def turn(j):
                        for u in range(2):
                            split_after(n0 + u, j, 2)
                            square(j * 2 + u, u, j)

                    turns(act, KT//2-1, turn)
                    for u in range(2):
                        square(KT - 2 + u, u, KT // 2 - 1)
                n0 += KT
                r0 += KT
            act.wait_ge(mean_v, 3)
            act.activation(rsb[:], rsb[:], ACT.Sqrt).then_inc(rstd_ok, 1)
            for k in range(KT):
                act.wait_ge(yt_ps, k + 1)
                b = 3 + k % 4
                A.add(act.activation(ytok[:, 0:2, k * P:k * P + P],
                                     ps[:, b, 0:256].rearrange("p (a d) -> p a d", a=2), ACT.Copy))
                act.activation(ytok[0:SMP, 2, k * P:k * P + P], ps[0:SMP, b, 256:384], ACT.Copy).then_inc(yt_ok, 1)

        @block.vector
        def _(dve):
            V = Count(dve, dv_c)
            TT, TS, STT = dve.tensor_tensor, dve.tensor_scalar, dve.scalar_tensor_tensor

            def split(n, slot):
                dve.wait_ge(hi_ready, n + 1)
                TT(wlo[:, slot], raw[:, slot], whi[:, slot].bitcast(F32), ALU.subtract).then_inc(lo_ready, 1)

            def split_after(n, i=None, per=0):
                if n + 2 < N_ALL:
                    split(n + 2 if i is None else i * per + (n + 2), n % 2)

            dve.memset(stat[:], 0.0).then_inc(stat_zero, 1)
            dve.wait_ge(stat_zero, 1)
            dve.wait_ge(ssq_ok, 1)
            V.add(TS(stat[:, 3:6], stat[:, 0:3], 1.0 / D, EPS, ALU.mult, ALU.add))
            V.sync()
            dve.reciprocal(stat[:, 3:6], stat[:, 3:6]).then_inc(rms_v, 1)
            dve.wait_ge(par_ok, 1)
            lb0, lb1 = prm[:, PR["lb"]][:, 0:8], prm[:, PR["lb"]][:, 8:16]
            V.add(TT(lbx[:, 4, :], lb0, lb1, ALU.max))
            V.sync()
            V.add(TT(lbx[:, 0, :], lb0, lbx[:, 4, :], ALU.subtract))
            TT(lbx[:, 1, :], lb1, lbx[:, 4, :], ALU.subtract).then_inc(rms_v, 1)
            dve.wait_ge(rsb_ok, 1)
            for k in range(KT):
                dve.wait_ge(xt_ok, k + 1)
                STT(hf[:, k, :], xT0[:, k, :], ln[:, 0, k:k + 1], rsb0[:], ALU.mult, ALU.mult).then_inc(hf_ok, 1)
            dve.wait_ge(rs_ok, 2)
            V.add(TT(lbx[:, 4, :], lbx[:, 2, :], lbx[:, 3, :], ALU.add))
            V.sync()
            V.add(dve.reciprocal(lbx[:, 5, :], lbx[:, 4, :]))
            V.sync()
            V.add(TT(lbx[:, 0, :], lbx[:, 2, :], lbx[:, 5, :], ALU.mult))
            V.sync()
            V.add(TS(lbx[:, 1, :], lbx[:, 0, :], -1.0, 1.0, ALU.mult, ALU.add))
            split(0, 0)
            split(1, 1)
            for k in range(KT):
                dve.wait_ge(hh_ok, k + 1)
                TT(hL[:, k, :], hf[:, k, :], hH[:, k, :].bitcast(F32), ALU.subtract).then_inc(hl_ok, 1)
            for n in range(4):
                split_after(n)
            dve.wait_ge(pe_ok, 1)
            dve.wait_ge(free[0], 2)
            dve.wait_ge(free[1], 2)
            TT(kcT[:, :, 0, :].rearrange("p c (r t) -> p c r t", r=2),
               kvq[:, 0:4, 0:SEQ].rearrange("p c (r t) -> p c r t", r=2),
               pe4[:].unsqueeze(2).to_broadcast([P, 4, 2, P]), ALU.add).then_inc(page_ok, 1)

            def turn(j):
                for u in range(4):
                    split_after(4 + u, j, 4)
                    dve.wait_ge(page_ps, j * 4 + (u + 1))
                    TT(kcT[:, :, ds(j * 2 + (1 + u // 2), 1), (u % 2) * P:(u % 2) * P + P],
                       ps[:, 4 + u, :].rearrange("p (c o t) -> p c o t", c=4, o=1),
                       pe4[:].unsqueeze(2), ALU.add).then_inc(page_ok, 1)

            turns(dve, N_A // 4 - 1, turn)
            split_after(N_GATE)
            for c in range(2):
                for q in range(4):
                    split_after(N_CMP + 4 * c + q)
                dve.wait_ge(hid_sg, c + 1)
                TT(hid[:, c, :], ps[:, c, 0:NCMP], hsg[:, c, :], ALU.mult).then_inc(hid_ok, 1)
            dve.wait_ge(gate_ok, 1)
            dve.wait_ge(cat_in, 16)
            V.add(TT(gate_p[:].rearrange("p t (h r) -> p t h r", r=3),
                     gates[:, 0:2, :].rearrange("p t (h r) -> p t h r", r=3),
                     cat_["valid"].rearrange("p (t o r) -> p t o r", t=2, o=1).to_broadcast([P, 2, HEADS, 3]), ALU.mult))
            dve.wait_ge(gsel_ps, 1)
            for k in range(4):
                c0 = (k % 2) * 24 + (k // 2) * 12
                V.add(TT(gtmp[:, k, :], ps[:, 1, c0:c0 + 12], cat_["head"], ALU.mult))
            V.sync()
            dve.tensor_reduce(gate_s[:], gtmp[:].rearrange("p k (h r) -> p k r h", r=3), X, ALU.add).then_inc(gsel_ok, 1)
            dve.wait_ge(gsel_ok, 1)

            def gate_step(par, m, n=N_MG):
                c = n + par + 2
                split(m * 2 + c, c % 2)

            PW = 512 + NCMP

            def scored(u, base, nk, src, bias, src_c, bias_c):
                row = 1 if base else 0
                dve.wait_ge(sc_ps, u + 1)
                V.add(TT(prob[:, base:base + 2 * nk].rearrange("p (b k) -> p b k", b=2), src, bias, ALU.add))
                TT(prob[:, base + 2 * nk:base + 2 * nk + NCMP], src_c, bias_c, ALU.add).then_inc(sc_rd, 1)
                V.sync()
                V.add(dve.tensor_reduce(nmax[:, row, 1:3],
                                        prob[:, base:base + 2 * nk].rearrange("p (b k) -> p b k", b=2), X, ALU.max,
                                        negate=True))
                dve.wait_ge(sc_rd, u + 1)
                dve.tensor_reduce(nmax[:, row, 0:1], prob[:, base + 2 * nk:base + 2 * nk + NCMP], X, ALU.max,
                                  negate=True).then_inc(nm_ok, 1)

            def weighted(u, base, nk, gate):
                row = 1 if base else 0
                dve.wait_ge(ex_ok, u + 1)
                V.add(dve.reciprocal(wgt[:, row, 0:3], sums[:, row, 0:3]))
                V.sync()
                V.add(TT(wgt[:, row, 0:3], wgt[:, row, 0:3], gate, ALU.mult))
                V.sync()
                for b in range(3):
                    w = prob[:, base + b * nk:base + (b + 1) * nk] if b < 2 else \
                        prob[:, base + 2 * nk:base + 2 * nk + NCMP]
                    ins = TS(w, w, wgt[:, row, BR[b]:BR[b] + 1], None, ALU.mult)
                    if b < 2:
                        V.add(ins)
                    else:
                        ins.then_inc(pn_ok, 1)

            for g in range(GROUPS):
                def turn(t):
                    for par in range(2):
                        h = t * 2 + (4 * g + par)
                        for qt in range(2):
                            nk = (qt + 1) * P
                            off = P if qt == 0 else 0
                            scored(h * 2 + qt, qt * PW, nk,
                                   ps[:, 2 + qt, 0:2 * nk].rearrange("p (b k) -> p b k", b=2),
                                   bias_p[:, ds(h, 1), off:off + nk].to_broadcast([P, 2, nk]),
                                   ps[:, 4, qt * NCMP:(qt + 1) * NCMP],
                                   bias_pc[:, qt, ds(h, 1), :].rearrange("p o k -> p (o k)"))
                        for qt in range(2):
                            weighted(h * 2 + qt, qt * PW, (qt + 1) * P, gate_p[:, qt, ds(h * 3, 3)])
                        gate_step(par, t + 2 * g)
                        dve.wait_ge(oh_ok, h + 1)
                        TT(oL[:, ds(h, 1), 0:SEQ], ps[:, 0:1, 0:SEQ], oH[:, ds(h, 1), 0:SEQ].bitcast(F32), ALU.subtract
                           ).then_inc(ol_ok, 1)
                turns(dve, HPG // 2, turn, V)
            for k in range(4):
                g, bh = k // 2, k % 2
                u = 16 + k
                gates_at = STACK_GATES[k]
                for at in gates_at[:3]:
                    for i in at:
                        gate_step(i % 2, i // 2)
                scored(u, 0, T, ps[:, 2:4, 0:T], bias_s[:, k:k + 1, :].to_broadcast([P, 2, T]), ps[:, 4, 0:NCMP],
                       bias_sc[:, k, :])
                weighted(u, 0, T, gate_s[:, k, :])
                for i in gates_at[3]:
                    gate_step(i % 2, i // 2)
                dve.wait_ge(oh_ok, HEADS + k + 1)
                for h4 in range(4):
                    sl = (slice(None), 4 * g + h4, slice(SEQ + 32 * bh, SEQ + 32 * bh + 32))
                    ins = TT(oL[sl].rearrange("p (j s) -> p j s", j=4),
                             ps[:, 0, 0:P].rearrange("p (j h s) -> p j h s", j=4, h=4)[:, :, h4, :],
                             oH[sl].bitcast(F32).rearrange("p (j s) -> p j s", j=4), ALU.subtract)
                    if h4 < 3:
                        V.add(ins)
                ins.then_inc(ol_ok, 1)

            lb, oml = lbx[:, 0, :], lbx[:, 1, :]

            def tail1(h):
                dve.wait_ge(t_ok, h + 1)
                for i in range(3):
                    m = P if i < 2 else SMP
                    ins = TT(vmask[0:m, i], v_tok[0:m, i:i + 1, :].to_broadcast([m, 8, P]),
                             c_("chunk_p" if i < 2 else "chunk_s")[0:m, :].unsqueeze(2).to_broadcast([m, 8, P]),
                             ALU.mult)
                    V.add(ins)
                mask = c_("causal_p").bitcast(U32)
                for i in range(2):
                    V.add(dve.copy_predicated(att[:, i * P:i * P + P], mask, ps[:, 4, i * P:i * P + P]))
                dve.copy_predicated(att[0:SMP, SEQ:T], c_("causal_s")[0:SMP, :].bitcast(U32),
                                    ps[0:SMP, 4, SEQ:T]).then_inc(m_ok, 1)

            def tail2(h, par, turn):
                if later(turn * 32):
                    dve.wait_ge(st_out[par], turn * 32)
                for c in range(16):
                    if c in (0, 8):
                        dve.wait_ge(u_ps, h * 3 + (1 if c == 0 else 2))
                    U = ps[:, (5, 6, 7, 2)[c // 4], (c % 4) * P:(c % 4) * P + P]
                    out = st[:, c + 1, :] if c < 15 else sfin[:, par, :]
                    if c == 0:
                        V.add(dve.tensor_copy(out, U))
                    else:
                        V.sync()
                        V.add(STT(out, st[:, c, :], cum[:, par, HC * c + HC - 1:HC * c + HC], U, ALU.mult, ALU.add))
                dve.wait_ge(u_ps, h * 3 + 3)
                dve.wait_ge(s0_in[par], turn * 16 + 16)
                for b in range(DB):
                    last = SEQ + DS * b + DS - 1
                    ins = STT(sn[:, par, b, :], s0[:, par, b, :], cum[:, par, last:last + 1],
                              ps[:, 3 + b // 4, (b % 4) * P:(b % 4) * P + P], ALU.mult, ALU.add)
                    if b < DB - 1:
                        V.add(ins)
                ins.then_inc(s_ok, 1)

            def tail3(h, par):
                dve.wait_ge(hm_ps, h + 1)
                V.add(TS(orn[:], ps[:, 6, 0:T], EPS, None, ALU.add))
                V.sync()
                dve.reciprocal(orn[:], orn[:]).then_inc(hv_ok, 1)
                dve.wait_ge(hr_ok, h + 1)
                V.add(STT(osb[:], osb[:], hgn, orn[:], ALU.mult, ALU.mult))
                V.sync()
                TT(osb[:], osb[:], ogs[:, par, :], ALU.mult).then_inc(hn_ok, 1)
                dve.wait_ge(hoh, h + 1)
                TT(oL[:, ds(h + 8, 1), :], osb[:].rearrange("p (o t) -> p o t", o=1),
                   oH[:, ds(h + 8, 1), :].bitcast(F32), ALU.subtract).then_inc(hol, 1)

            def window(h, par, i=None, k=0):
                n = N_HG + 4 * k
                nn = n if i is None else i * 8 + n
                turn = (k - 1) // 2 if i is None else i + (k - 1) // 2
                if k:
                    tail1(h - 1)
                split_after(n, i, 8)
                if k:
                    tail2(h - 1, 1 - par, turn)
                dve.wait_ge(free[0], h * 2 + (R_HG // 2 + 1))
                V.add(TS(fsig[:], fsig[:], oml[:, ds(h, 1)], lb[:, ds(h, 1)], ALU.mult, ALU.add))
                V.add(TS(nsig[:], nsig[:], oml[:, ds(h, 1)], None, ALU.mult))
                V.sync()
                V.add(TT(fmul[:], fsig[:], c_("seg"), ALU.mult))
                V.sync()
                V.add(TT(fset[:], fsig[:], fmul[:], ALU.subtract))
                V.sync()
                V.add(dve.tensor_tensor_scan(cum[:, par, :], fmul[:], fset[:], 0.0, ALU.mult, ALU.add))
                V.sync()
                V.add(dve.reciprocal(fmul[:], cum[:, par, :]))
                V.sync()
                V.add(TT(kinv[:, par, :], nsig[:], fmul[:], ALU.mult))
                V.sync()
                V.add(TT(kend[:, par, 0:SEQ].rearrange("p (c s) -> p c s", s=HC),
                         kinv[:, par, 0:SEQ].rearrange("p (c s) -> p c s", s=HC),
                         cum[:, par, 0:SEQ].rearrange("p (c s) -> p c s", s=HC)[:, :, HC - 1:HC].to_broadcast([P, 16, HC]),
                         ALU.mult))
                TT(kend[:, par, SEQ:T].rearrange("p (c s) -> p c s", s=DS),
                   kinv[:, par, SEQ:T].rearrange("p (c s) -> p c s", s=DS),
                   cum[:, par, SEQ:T].rearrange("p (c s) -> p c s", s=DS)[:, :, DS - 1:DS].to_broadcast([P, DB, DS]),
                   ALU.mult).then_inc(f_done, 1)
                split_after(n + 1, i, 8)
                split_after(n + 2, i, 8)
                TT(qdec[:, par, :], ps[:, 0, 0:T], cum[:, par, :], ALU.mult).then_inc(free[0], 1)
                if k:
                    tail3(h - 1, 1 - par)
                split_after(n + 3, i, 8)
                dve.wait_ge(o_sig, h + 1)
                TT(ogs[:, par, :], ps[:, 1, 0:T], osig[:], ALU.mult).then_inc(free[1], 1)

            dve.wait_ge(kv_out, 16 * 13)
            V.add(dve.memset(att[:], 0.0))
            V.sync()
            window(0, 0)
            window(1, 1, None, 1)
            window(2, 0, None, 2)
            with V.loop(2, 2 * (8 + 5 + 23 + 2)) as i:
                window(i * 2 + 3, 1, i, 3)
                window(i * 2 + 4, 0, i, 4)
            window(7, 1, None, 7)
            late = [(i % 2, M_LATE + i // 2, N_MG2 - 2 * M_LATE) for i in range(4)]
            tail1(7)
            gate_step(*late[0])
            tail2(7, 1, 3)
            gate_step(*late[1])
            tail3(7, 1)
            gate_step(*late[2])
            gate_step(*late[3])

            for par in range(2):
                dve.wait_ge(st_out[par], 16 * HEADS)
            for par in range(2):
                dve.wait_ge(spilled[par], 16 * KT)
            dve.wait_ge(hoh, HEADS)

            def turn(j):
                for v in range(2):
                    m = j * 2 + v
                    dve.wait_ge(sg_in[v], j * 16 + 16)
                    dve.wait_ge(used, m + (N_AB + 1))
                    if later(m):
                        dve.wait_ge(mg_lo, m)
                    V.add(TT(mix[:, v, :], sg[:, v, 0, :], ps[:, 4 * v + 2, 0:T], ALU.mult))
                    TT(mix2[:, v, :], sg[:, v, 1, :], ps[:, 4 * v + 3, 0:T], ALU.mult).then_inc(mg_rd[v], 1)
                    V.sync()
                    dve.wait_ge(mg_rd[v], j + 1)
                    TT(mix[:, v, :], mix[:, v, :], mix2[:, v, :], ALU.add).then_inc(mg_mix, 1)
                    split(m + (N_AB + 2), (N_AB + v) % 2)
                    dve.wait_ge(mg_hi, m + 1)
                    TT(mL[:, ds(m, 1), :], mix[:, v:v + 1, :], mH[:, ds(m, 1), :].bitcast(F32), ALU.subtract
                       ).then_inc(mg_lo, 1)

            turns(dve, KT // 2, turn, V)
            V.add(dve.memset(sqs[:], 0.0))
            V.sync()
            def turn(j):
                for u in range(2):
                    m = j * 2 + u
                    split_after(N_OUT + u, j, 2)
                    dve.wait_ge(y_sq, m + 1)
                    if later(m):
                        dve.wait_ge(y_add, m)
                    TT(sqs[:], sqs[:], sq[:, u, :], ALU.add).then_inc(y_add, 1)

            turns(dve, KT//2, turn)

            def rstd(k):
                dve.wait_ge(mean_ps if k != 2 else x_add, {1: 1, 2: KT, 3: 2}[k])
                V.add(TS(rsb[:], ps[:, 2, 0:T], EPS, None, ALU.add))
                V.add(dve.memset(sqs[:], 0.0))
                V.sync()
                dve.reciprocal(rsb[:], rsb[:]).then_inc(mean_v, 1)
                dve.wait_ge(rstd_ok, k)

            def normed(out, in_, n, k):
                V.add(STT(out[:, k, :], in_[:, k, :], ln[:, n, k:k + 1], rsb[:], ALU.mult, ALU.mult))
                V.sync()

            rstd(1)
            dve.wait_ge(x1_in, 16)
            dve.wait_ge(free[0], R_FFN // 2)
            dve.wait_ge(free[1], R_FFN // 2)
            V.add(TT(y1[:, 0, :], y1[:, 0, :], rsb[:], ALU.mult))
            for k in range(KT):
                V.sync()
                if k < KT - 1:
                    V.add(TT(y1[:, k + 1, :], y1[:, k + 1, :], rsb[:], ALU.mult))
                TT(x1[:, k, :], x1[:, k, :], y1[:, k, :], ALU.add).then_inc(x_new, 1)
            rstd(2)
            for k in range(KT + 1):
                if k < KT:
                    STT(y1[:, k, :], x1[:, k, :], ln[:, 2, k:k + 1], rsb[:], ALU.mult, ALU.mult).then_inc(h_new, 1)
                if k:
                    dve.wait_ge(h2h, k)
                    TT(hL[:, k - 1, :], y1[:, k - 1, :], hH[:, k - 1, :].bitcast(F32), ALU.subtract).then_inc(h2l, 1)

            dve.wait_ge(hist_ok, 4)
            dve.wait_ge(h2l, KT)
            V.add(dve.memset(ue[:, :, :, 0:2], 0.0))
            V.sync()
            n0, r0, i0 = N_FFN, R_FFN, 0
            for part, cnt in enumerate(PARTS):
                def turn(j):
                    for par in range(2):
                        i = j * 2 + (i0 + par)
                        for s in range(2):
                            dve.tensor_copy(ue[:, par, s, 2 + SEQ:UW].rearrange("p (b c) -> p b c", b=DB)[:, :, 0:2],
                                            hist[:, ds(i + s * FT, 1), :].rearrange("p o (b c) -> p (o b) c", b=DB)
                                            ).then_inc(u_hist, 1)
                        for s in range(2):
                            col = i + s * FT
                            split_after(n0 + 2 * par + s, j, 4)
                            dve.wait_ge(u_ev, i * 2 + (s + 1))
                            V.add(STT(cc[:, s, :], ue[:, par, s, 1:UW - 1], conv[:, 1, ds(col, 1)], cc[:, s, :],
                                      ALU.mult, ALU.add))
                            V.sync()
                            STT(cc[:, s, :], ue[:, par, s, 2:UW], conv[:, 2, ds(col, 1)], cc[:, s, :],
                                ALU.mult, ALU.add).then_inc(c_ok, 1)
                            V.add(dve.tensor_copy(newc[:, ds(col, 1), :].rearrange("p o (b c) -> p (o b) c", b=NSEQ),
                                                  ue[:, par, s, UW - 90:UW].rearrange("p (b c) -> p b c", b=NSEQ)[:, :, 8:]))
                        dve.wait_ge(g_ok, i + 1)
                        if later(i):
                            dve.wait_ge(a_hi, i)
                        V.add(TT(gg[:, 0:SEQ], cc[:, 0, 0:SEQ], cc[:, 1, 0:SEQ], ALU.mult))
                        TT(gg[:, SEQ:T].rearrange("p (b c) -> p b c", b=DB),
                           cc[:, 0, SEQ:UW - 2].rearrange("p (b c) -> p b c", b=DB)[:, :, 2:],
                           cc[:, 1, SEQ:UW - 2].rearrange("p (b c) -> p b c", b=DB)[:, :, 2:], ALU.mult
                           ).then_inc(m_new, 1)
                        dve.wait_ge(a_hi, i + 1)
                        TT(aL[:, ds(j * 2 + par, 1), :], gg[:].rearrange("p (o t) -> p o t", o=1),
                           aH[:, ds(j * 2 + par, 1), :].bitcast(F32), ALU.subtract).then_inc(a_lo, 1)

                turns(dve, cnt//2, turn, V)
                n0 += 2 * cnt
                r0 += 2 * cnt
                i0 += cnt

                def down(m, u, j, last):
                    dve.wait_ge(used, m + (n0 + 1))
                    tile = acc[:, ds(m, 1), :]
                    if part == 0:
                        dve.tensor_copy(tile, ps[:, u:u + 1, 0:T]).then_inc(free[u], 1)
                    else:
                        TT(tile, tile, ps[:, u:u + 1, 0:T], ALU.add).then_inc(free[u], 1)
                    if part == 2:
                        dve.wait_ge(d_sq, m + 1)
                        if later(m):
                            dve.wait_ge(d_add, m)
                        TT(sqs[:], sqs[:], sq[:, u, :], ALU.add).then_inc(d_add, 1)

                def turn(j):
                    for u in range(2):
                        split_after(n0 + u, j, 2)
                        down(j * 2 + u, u, j, False)

                turns(dve, KT//2-(part==2), turn)
                if part == 2:
                    for u in range(2):
                        down(KT - 2 + u, u, KT // 2 - 1, True)
                n0 += KT
                r0 += KT
            rstd(3)
            for k in range(KT):
                normed(acc, acc, 3, k)
                TT(acc[:, k, :], acc[:, k, :], x1[:, k, :], ALU.add).then_inc(y_fin, 1)

        @block.tensor
        def _(pe):
            def product(out, lhsT, rhs, start=True, stop=True):
                return pe.matmul(out, lhsT, rhs, start=start, stop=stop, skip_group_check=True)

            def gemm(n, slot, out, xH, xL, tiles, wait=True, done=True, start=True, stop=True):
                if wait:
                    pe.wait_ge(lo_ready, n + 1)
                last = len(tiles) - 1
                for q, (w, k) in enumerate(tiles):
                    for p_, (ww, xx) in enumerate(((whi, xH), (whi, xL), (wlo, xH))):
                        ins = pe.matmul(out, ww[:, slot, w, :], xx[:, k, :],
                                        start=(start and q == 0 and p_ == 0), stop=(stop and q == last and p_ == 2),
                                        skip_group_check=True)
                if done:
                    ins.then_inc(used, 1)
                return ins

            all16 = [(k, k) for k in range(16)]

            pe.wait_ge(cst_in, 16)
            pe.wait_ge(rows_in, 16 * 8)
            pe.transpose(ps[:, 1, 0:81], rows[0:81, :], ident[0:81, 0:81])
            for n in range(4):
                ins = pe.transpose(ps[:, 1, 81 + 88 * n:81 + 88 * n + 88], crow[:, n, :], ident[0:88, 0:88])
            ins.then_inc(par_ps, 1)
            pe.wait_ge(pe_in, 16)
            for c in range(2):
                pe.transpose(ps[:, 0, T + c * BLK:T + c * BLK + BLK], pe_row[:, c, :], ident[0:BLK, 0:BLK])
            pe.wait_ge(x_in, 48)
            for k in range(KT):
                if k >= 6:
                    pe.wait_ge(xt_ok, k - 5)
                for i in range(3):
                    m = P if i < 2 else SMP
                    ins = pe.transpose(ps[:, 2 + k % 6, i * P:i * P + m], xtok[0:m, i, k * P:k * P + P],
                                       ident[0:m, 0:m])
                ins.then_inc(xt_ps, 1)
                if k == 5:
                    pe.wait_ge(rs_ok, 1)
                    for i in range(3):
                        m = P if i < 2 else SMP
                        ins = product(ps[:, 0, i * P:i * P + m], stat[0:m, 3 + i:4 + i].to_broadcast([m, P]),
                                      ident[0:m, 0:m])
                    ins.then_inc(rsb_ps, 1)
            pe.wait_ge(hl_ok, KT)
            pe.wait_ge(par_ok, 1)
            pe.wait_ge(rsb_ok, 1)
            pe.wait_ge(pe_ok, 1)
            for n in range(4):
                if n >= 2:
                    pe.wait_ge(free[n % 2], 1)
                gemm(n, n % 2, ps[:, n % 2, 0:T], hH, hL, all16)

            def turn(j):
                for u in range(4):
                    pe.wait_ge(free[u % 2], j * 2 + (1 + (u + 2) // 2))
                    gemm(j * 4 + (4 + u), u % 2, ps[:, u % 2, 0:T], hH, hL, all16)
                    pe.wait_ge(page_in[u], j * 16 + 16)
                    if later(j):
                        pe.wait_ge(page_ok, j * 4 + (u - 2))
                    for c in range(4):
                        ins = pe.transpose(ps[:, 4 + u, c * P:c * P + P], page[:, u, c * P:c * P + P], ident)
                    ins.then_inc(page_ps, 1)

            turns(pe, N_A // 4 - 1, turn)
            pe.wait_ge(lo_ready, N_GATE + 1)
            for k in range(KT):
                for p_, (ww, xx) in enumerate(((whi, hH), (whi, hL), (wlo, hH))):
                    ins = product(ps[0:24, 2, 0:T], ww[:, N_GATE % 2, k, 0:24], xx[:, k, :],
                                  start=(k == 0 and p_ == 0), stop=(k == 15 and p_ == 2))
            ins.then_inc(used, 1)
            pe.wait_ge(free[0], N_A // 2)
            pe.wait_ge(free[1], N_A // 2)
            pe.wait_ge(page_ok, 17)
            blocks = kcT[:].rearrange("p (c g) s (b l) -> p c l (g s b)", c=2, l=BLK)
            for c in range(2):
                for q in range(4):
                    n = N_CMP + 4 * c + q
                    pe.wait_ge(loaded[n % 2], n // 2 * 16 + 16)
                    for l in range(16):
                        ins = product(ps[:, c, 0:NCMP], raw[:, n % 2, l, :], blocks[:, c, 16 * q + l, :],
                                      start=(q == 0 and l == 0), stop=(q == 3 and l == 15))
                    ins.then_inc(used, 1)
                    if n == N_CMP:
                        pe.wait_ge(gate_f, 1)
                        for i, t0 in enumerate((0, P, T - P)):
                            ins = pe.transpose(ps[:, 2, i * 24:i * 24 + 24], mgate[0:24, 0, t0:t0 + P], ident[0:24, 0:24])
                        ins.then_inc(gate_t, 1)
            for f in range(12):
                if f >= 4:
                    pe.wait_ge(tok_ok, f - 3)
                for i in range(3):
                    m = P if i < 2 else SMP
                    ins = pe.transpose(ps[0:m, 4 + f % 4, i * P:i * P + P], kvq[:, f, i * P:i * P + m], ident)
                ins.then_inc(tok_ps, 1)
                if f == 3:
                    pe.wait_ge(w2_in, 16)
                    pe.wait_ge(hid_ok, 2)
                    pe.wait_ge(gate_ok, 1)
                    product(ps[:, 2, 0:NCMP], w2[:, 0, :], hid[:, 0, :])
                    product(ps[0:NCMP, 3, 0:P], hid[:, 1, :], w2[:, 1, :]).then_inc(cc_ps, 1)
            pe.wait_ge(cat_in, 16)
            for bh in range(2):
                ins = product(ps[:, 1, bh * 24:bh * 24 + 24], pick[:, bh, :], gates[:, 2, :])
            ins.then_inc(gsel_ps, 1)
            pe.wait_ge(tok_ok, 12)
            pe.wait_ge(cc_ok, 2)
            pe.wait_ge(gsel_ok, 1)

            def merge_gate(par, m, part=0, n=N_MG, bank=None):
                if part < 2 and later(m):
                    pe.wait_ge(gs_rd[par], m)
                tiles = (all16, all16[:12], all16[12:])[part]
                gemm(m * 2 + (n + par), (N_MG + par) % 2, ps[:, 1 + 4 * par if bank is None else bank, 0:T], hH, hL,
                     tiles, wait=(part < 2), done=(part != 1), start=(part < 2), stop=(part != 1))

            PW = 512 + NCMP
            for g in range(GROUPS):
                def turn(t):
                    for par in range(2):
                        h = t * 2 + (4 * g + par)
                        pe.wait_ge(q_ok, h + 1)
                        if later(h):
                            pe.wait_ge(sc_rd, h * 2)
                        for qt in range(2):
                            product(ps[:, 4, qt * NCMP:(qt + 1) * NCMP], qst[:, par, qt * P:qt * P + P], ckT[:])
                        for qt in range(2):
                            nk = (qt + 1) * P
                            q = qst[:, par, qt * P:qt * P + P]
                            product(ps[:, 2 + qt, 0:nk], q, kvq[:, 4 + g, 0:nk])
                            product(ps[:, 2 + qt, nk:2 * nk], q, kvq[:, 8 + g, 0:nk]).then_inc(sc_ps, 1)
                        merge_gate(par, t + 2 * g, 1)
                        for qt in range(2):
                            base, nb = qt * PW, 2 * (qt + 1)
                            pe.wait_ge(pn_ok, h * 2 + (qt + 1))
                            if later(h * 2 + qt):
                                pe.wait_ge(pt_ok, h * 2 + qt)
                            for b in range(nb):
                                pe.transpose(ps[:, 6, b * P:b * P + P], prob[:, base + b * P:base + b * P + P], ident)
                            pe.transpose(ps[0:NCMP, 7, 0:P], prob[:, base + nb * P:base + nb * P + NCMP], ident
                                         ).then_inc(pt_ps, 1)
                            if qt == 0:
                                merge_gate(par, t + 2 * g, 2)
                        if later(h):
                            pe.wait_ge(ol_ok, h)
                        for qt in range(2):
                            pe.wait_ge(pt_ok, h * 2 + (qt + 1))
                            out = ps[:, 0, qt * P:qt * P + P]
                            for br, col in enumerate((6 + g, 10 + g)):
                                for kt in range(qt + 1):
                                    product(out, kvtok[:, kt, col * P:col * P + P], pT[qt][:, br * (qt + 1) + kt, :],
                                            start=(br == 0 and kt == 0), stop=False)
                            ins = product(out, cv[0:NCMP, :], pTc[0:NCMP, qt, :], start=False)
                        ins.then_inc(ov_ps, 1)
                turns(pe, HPG // 2, turn)
            pe.wait_ge(q_ok, HEADS + 1)
            for k in range(4):
                g, u = k // 2, 16 + k
                gates_at = STACK_GATES[k]
                for i in gates_at[0]:
                    merge_gate(i % 2, i // 2)
                pe.wait_ge(sc_rd, u)
                pe.wait_ge(pt_ok, u)
                for br, (kv, arrived) in enumerate(((kv_sel, sel_in), (kv_win, win_in))):
                    pe.wait_ge(arrived, 128 * (k + 1))
                    for j in range(4):
                        for t in range(2):
                            b = 2 * j + t
                            ins = pe.transpose(ps[:, 6 + b // 4, (b % 4) * P:(b % 4) * P + P], kv[:, j, 2 * t, :], ident)
                    ins.then_inc(kt_ps, 1)
                    for i in gates_at[1 + br]:
                        merge_gate(i % 2, i // 2)
                    pe.wait_ge(kt_ok, 2 * k + br + 1)
                    for j in range(4):
                        product(ps[32 * j:32 * j + 32, 2 + br, 0:PAST], qs[:, k, 32 * j:32 * j + 32],
                                KTs[:, 2 * j:2 * j + 2, :].rearrange("p a d -> p (a d)"))
                    product(ps[:, 2 + br, PAST:T], qs[:, k, :], kvq[:, (4, 8)[br] + g, SEQ:T]).then_inc(ks_ps, 1)
                product(ps[:, 4, 0:NCMP], qs[:, k, :], ckT[:]).then_inc(sc_ps, 1)
                for i in gates_at[3]:
                    merge_gate(i % 2, i // 2)
                pe.wait_ge(pn_ok, u + 1)
                for br in range(2):
                    for t in range(3):
                        m = P if t < 2 else SMP
                        pe.transpose(ps[0:m, 6 + br, t * P:t * P + P], prob[:, br * T + t * P:br * T + t * P + m], ident)
                pe.transpose(ps[0:NCMP, 7, 384:512], prob[:, 2 * T:2 * T + NCMP], ident).then_inc(pt_ps, 1)
                pe.wait_ge(pt_ok, u + 1)
                pe.wait_ge(ol_ok, HEADS + k)
                for br, col in enumerate((6 + g, 10 + g)):
                    product(ps[:, 0, 0:P], kvtok[0:SMP, 2, col * P:col * P + P], pTs[0:SMP, 3 * br + 2, :],
                            start=(br == 0), stop=False)
                product(ps[:, 0, 0:P], cv[0:NCMP, :], pTs[0:NCMP, 6, :], start=False, stop=False)
                for br, kv in enumerate((kv_sel, kv_win)):
                    for j in range(4):
                        for t in range(2):
                            ins = product(ps[:, 0, 32 * j:32 * j + 32], kv[:, j, 2 * t + 1, :],
                                          pTs[:, 3 * br + t, 32 * j:32 * j + 32], start=False,
                                          stop=(br == 1 and t == 1))
                ins.then_inc(ov_ps, 1)

            def tail1(h, par):
                pe.wait_ge(f_done, h + 1)
                pe.wait_ge(free[1], h * 2 + (R_HG // 2 + 1))
                pe.wait_ge(free[0], h * 2 + (R_HG // 2 + 2))
                if later(h):
                    pe.wait_ge(s_ok, h)
                for bank, src in ((2, kend), (3, vT)):
                    for i in range(3):
                        m = P if i < 2 else SMP
                        pe.transpose(ps[0:m, bank, i * P:i * P + P], src[:, par, i * P:i * P + m], ident)
                for i in range(3):
                    m = P if i < 2 else SMP
                    sl = slice(i * P, i * P + m)
                    ins = product(ps[0:m, 4, sl], kinv[:, par, sl], qdec[:, par, sl])
                ins.then_inc(t_ps, 1)

            def tail2(h):
                pe.wait_ge(m_ok, h + 1)
                if later(h):
                    pe.wait_ge(ho_sb, h)
                if later(h):
                    pe.wait_ge(hv_ok, h)
                for i, banks in enumerate(((5, 6), (7, 2), (3, 4))):
                    m = P if i < 2 else SMP
                    for q, bank in enumerate(banks):
                        ins = product(ps[:, bank, :], kend_tok[0:m, i, :],
                                      vmask[0:m, i, 4 * q:4 * q + 4, :].rearrange("p c d -> p (c d)"))
                    ins.then_inc(u_ps, 1)

            def tail3(h, par):
                pe.wait_ge(s_ok, h + 1)
                for i in range(3):
                    m = P if i < 2 else SMP
                    sl = slice(i * P, i * P + m)
                    product(ps[:, 5, sl], v_tok[0:m, i, :], att[0:m, sl], start=(i == 0), stop=False)
                for c in range(1, 16):
                    sl = slice(HC * c, HC * c + HC)
                    product(ps[:, 5, sl], st[:, c, :], qdec[:, par, sl], start=False, stop=False)
                for b in range(DB):
                    sl = slice(SEQ + DS * b, SEQ + DS * b + DS)
                    ins = product(ps[:, 5, sl], s0[:, par, b, :], qdec[:, par, sl], start=False, stop=(b == DB - 1))
                ins.then_inc(ho_ps, 1)

            def tail4(h):
                pe.wait_ge(ho_sb, h + 1)
                product(ps[:, 6, 0:T], c_("mean_h"), osq[:]).then_inc(hm_ps, 1)

            def window(h, par, i=None, k=0):
                n = N_HG + 4 * k
                nn = n if i is None else i * 8 + n
                if k:
                    tail1(h - 1, 1 - par)
                for u in range(4):
                    pe.wait_ge(free[u % 2], h * 2 + (R_HG // 2 + u // 2))
                    gemm(nn + u, (n + u) % 2, ps[:, u % 2, 0:T], hH, hL, all16)
                    if k and u == 0:
                        tail2(h - 1)
                    if k and u == 1:
                        tail3(h - 1, 1 - par)
                    if k and u == 2:
                        tail4(h - 1)

            pe.wait_ge(ol_ok, HEADS + 4)
            for par in range(2):
                pe.wait_ge(gs_rd[par], M_LATE)
            window(0, 0)
            window(1, 1, None, 1)
            window(2, 0, None, 2)
            with pe.Fori(0, 2) as i:
                window(i * 2 + 3, 1, i, 3)
                window(i * 2 + 4, 0, i, 4)
            window(7, 1, None, 7)
            late = [(i % 2, M_LATE + i // 2, 0, N_MG2 - 2 * M_LATE, i % 2) for i in range(4)]
            tail1(7, 1)
            pe.wait_ge(free[0], R_OUT // 2)
            pe.wait_ge(free[1], R_OUT // 2)
            merge_gate(*late[0])
            tail2(7)
            merge_gate(*late[1])
            tail3(7, 1)
            merge_gate(*late[2])
            tail4(7)
            merge_gate(*late[3])

            pe.wait_ge(hv_ok, HEADS)
            pe.wait_ge(s_ok, HEADS)

            def turn(j):
                for v in range(2):
                    n = N_AB + v
                    if later(j):
                        pe.wait_ge(mg_rd[v], j)
                    gemm(j * 2 + n, n % 2, ps[:, 4 * v + 2, 0:T], oH, oL, [(k, k) for k in range(8)], done=False)
                    if not later(j) and v == 0:
                        pe.wait_ge(hol, HEADS)
                    gemm(j * 2 + n, n % 2, ps[:, 4 * v + 3, 0:T], oH, oL, [(k, k) for k in range(8, 16)], wait=False)

            turns(pe, KT // 2, turn)
            for par in range(2):
                pe.wait_ge(gs_rd[par], KT)
            def turn(j):
                for u in range(2):
                    pe.wait_ge(free[u], j + R_OUT // 2)
                    if not later(j) and u == 0:
                        pe.wait_ge(mg_lo, KT - 1)
                        gemm(N_OUT, N_OUT % 2, ps[:, 0, 0:T], mH, mL, all16[:-1], done=False, stop=False)
                        pe.wait_ge(mg_lo, KT)
                        gemm(N_OUT, N_OUT % 2, ps[:, 0, 0:T], mH, mL, all16[-1:], wait=False, start=False)
                    else:
                        gemm(j * 2 + (N_OUT + u), (N_OUT + u) % 2, ps[:, u, 0:T], mH, mL, all16)

            turns(pe, KT//2, turn)
            pe.wait_ge(y_add, KT)
            product(ps[:, 2, 0:T], c_("mean_d"), sqs[:]).then_inc(mean_ps, 1)
            pe.wait_ge(hrow_in, 16)
            for i in range(4):
                for q in range(4):
                    ins = pe.transpose(ps[:, 3 + i, q * 2 * FT:(q + 1) * 2 * FT], hrow[:, 4 * i + q, :],
                                       ident[0:2 * FT, 0:2 * FT])
                ins.then_inc(hist_ps, 1)
            pe.wait_ge(mean_v, 1)
            for k in range(KT):
                pe.wait_ge(x_sq, k + 1)
                ins = product(ps[:, 2, 0:T], c_("mean_d"), sq[:, k % 2, :], start=(k == 0), stop=(k == KT - 1))
                ins.then_inc(x_add, 1)
            n0, r0, i0 = N_FFN, R_FFN, 0
            for part, cnt in enumerate(PARTS):
                def turn(i):
                    for s in range(2):
                        pe.wait_ge(free[s], i + r0 // 2)
                        if part == 0 and s == 0 and not later(i):
                            for k in range(KT):
                                pe.wait_ge(h2l, k + 1)
                                gemm(n0, n0 % 2, ps[:, 0, 0:T], hH, hL, all16[k:k + 1], wait=(k == 0),
                                     done=(k == KT - 1), start=(k == 0), stop=(k == KT - 1))
                        else:
                            gemm(i * 2 + (n0 + s), (n0 + s) % 2, ps[:, s, 0:T], hH, hL, all16)

                turns(pe, cnt, turn)
                n0 += 2 * cnt
                r0 += 2 * cnt
                i0 += cnt
                if part == 2:
                    pe.wait_ge(hist_ok, 4)
                    pe.wait_ge(a_lo, i0)
                    for i in range(5):
                        for q in range(4 * i, min(4 * i + 4, 2 * NSEQ)):
                            ins = pe.transpose(ps[0:2 * FT, 3 + i, (q - 4 * i) * P:(q - 4 * i + 1) * P],
                                               newc[:, :, q], ident)
                        ins.then_inc(nc_ps, 1)
                def turn(j):
                    for u in range(2):
                        pe.wait_ge(free[u], j + r0 // 2)
                        tiles = [(k, k) for k in range(cnt)]
                        if not later(j) and u == 0:
                            pe.wait_ge(a_lo, i0 - 1)
                            gemm(n0, n0 % 2, ps[:, 0, 0:T], aH, aL, tiles[:-1], done=False, stop=False)
                            pe.wait_ge(a_lo, i0)
                            gemm(n0, n0 % 2, ps[:, 0, 0:T], aH, aL, tiles[-1:], wait=False, start=False)
                        else:
                            gemm(j * 2 + (n0 + u), (n0 + u) % 2, ps[:, u, 0:T], aH, aL, tiles)

                turns(pe, KT//2, turn)
                n0 += KT
                r0 += KT
            pe.wait_ge(d_add, KT)
            product(ps[:, 2, 0:T], c_("mean_d"), sqs[:]).then_inc(mean_ps, 1)
            pe.wait_ge(nc_ok, 5)
            for k in range(KT):
                pe.wait_ge(y_fin, k + 1)
                if k >= 4:
                    pe.wait_ge(yt_ok, k - 3)
                for i in range(3):
                    m = P if i < 2 else SMP
                    ins = pe.transpose(ps[0:m, 3 + k % 4, i * P:i * P + P], acc[:, k, i * P:i * P + m], ident)
                ins.then_inc(yt_ps, 1)


def constants():
    import numpy as np

    def put(out, spec, name, value):
        v = np.asarray(value, np.float32)
        v = v.reshape(v.shape[0], -1)
        out[:v.shape[0], spec[name]] = v

    p = np.arange(P)
    t = np.arange(T)
    c = np.zeros((P, CP_N), np.float32)
    put(c, CP, "ident", np.eye(P))
    put(c, CP, "mean_d", np.full((P, P), 1.0 / D))
    put(c, CP, "mean_h", np.full((P, P), 1.0 / P))
    starts = np.where(t < SEQ, t % HC == 0, (t - SEQ) % DS == 0)
    put(c, CP, "seg", np.broadcast_to(1.0 - starts, (P, T)))
    put(c, CP, "causal_p", (p[:, None] // HC == p // HC) & (p[:, None] <= p))
    s = np.arange(SMP)
    put(c, CP, "causal_s", (s[:, None] // DS == s // DS) & (s[:, None] <= s))
    put(c, CP, "chunk_p", p[:, None] // HC == np.arange(8))
    put(c, CP, "chunk_s", s[:, None] // DS == np.arange(8))

    a = np.zeros((P, CA_N), np.float32)
    slope = 2.0 ** -(np.arange(HEADS) + 1.0)

    def bias(slopes, dist, ok):
        return np.where(ok & (dist >= 0), -slopes * dist, NEG)

    dist = p[:, None] - (np.arange(2 * P) - P)
    put(a, CA, "bias_p", bias(slope[None, :, None], dist[:, None, :], True))
    g, q, b = np.meshgrid(np.arange(GROUPS), np.arange(NSEQ), np.arange(NBLK), indexing="ij")
    g, q, end = g.ravel(), q.ravel(), (b.ravel() + 1) * BLK - 1
    pos = np.arange(2)[None, :] * P + p[:, None]
    put(a, CA, "bias_pc", bias(slope[None, None, :, None], (pos[:, :, None] - end)[:, :, None, :],
                               (q == 0) & (g == (np.arange(HEADS) // HPG)[:, None])))
    put(a, CA, "valid", np.stack([pos >= BLK - 1, pos >= 0, pos >= 0], -1))
    j, hh, ss = p // 32, p // DS % HPG, p % DS
    bs, bsc = [], []
    for k in range(4):
        gk, seq = k // 2, 4 * (k % 2) + j
        sl = slope[4 * gk + hh][:, None]
        bs.append(np.concatenate([bias(sl, PAST + ss[:, None] - np.arange(PAST), True),
                                  bias(sl, ss[:, None] - s % DS, s // DS == seq[:, None])], 1))
        bsc.append(bias(sl, PAST + ss[:, None] - end, (g == gk) & (q == 1 + seq[:, None])))
    put(a, CA, "bias_s", np.stack(bs, 1))
    put(a, CA, "bias_sc", np.stack(bsc, 1))
    rows = p[:, None] - (P - SMP)
    put(a, CA, "pick", np.stack([rows == (4 * bh + j) * DS + ss for bh in range(2)], 1))
    put(a, CA, "head", np.broadcast_to(hh[:, None, None] == np.arange(4)[:, None], (P, 4, 3)))
    return c, a


_OUTS = [(1, SEQ, D), (DB, DS, D)] + [s for _ in range(2) for s in
                                      ((1, 1, SEQ, 2, GROUPS, P), (1, DB, DS, 2, GROUPS, P))] + [
    (1, 1, SEQ, 2, GROUPS, P), (1, DB, PAST, 2, GROUPS, P),
    (1, 1, HEADS, P, P), (1, DB, HEADS, P, P), (1, 1, 2, 2 * DFF), (1, DB, 2, 2 * DFF)]


def kernel(**inputs):
    import numpy as np
    import concourse.bacc as bacc
    from concourse.bass_utils import run_bass_kernel_spmd as run

    nc = bacc.Bacc("TRN2", target_bir_lowering=False, num_devices=1)
    const, att_const = constants()
    arrays, aps = {}, {}
    for name, v in {**inputs, "const": const, "att_const": att_const}.items():
        v = np.ascontiguousarray(v)
        arrays[f"in_{name}"] = v
        aps[name] = nc.dram_tensor(f"in_{name}", v.shape, mybir.dt.from_np(v.dtype), kind="ExternalInput").ap()
    outs = [nc.dram_tensor(f"out_{i}", shape, F32, kind="ExternalOutput").ap() for i, shape in enumerate(_OUTS)]
    xt = nc.dram_tensor("x_feature_major", (P, KT * T), F32, kind="Internal").ap()
    gate = nc.dram_tensor("merge_gates", (KT, 2, P, T), F32, kind="Internal").ap()
    layer(nc, aps, outs, xt, gate)
    r = run(nc, [arrays], core_ids=[0])
    return tuple(r.results[0][f"out_{i}"] for i in range(len(_OUTS)))
```
